# Optimizing a Trainium2 kernel written in Bass

```python
import jax, jax.numpy as jnp
from jax import lax
import numpy as np

D_MODEL = 1024
BATCH = 1
SEQ = 512
DEPTH = 2

GRID_W = 64
CTX_LEN = 256
E_CONV = 768
CONV_WIDTH = 31
E_FOURIER = 512
FOURIER_GROUPS = 4
E_REC = 768
REC_HEADS = 6
REC_KEY = E_REC // REC_HEADS
REC_VAL = E_REC // REC_HEADS
CHUNK = 32
N_BRANCH = 3
EPS = 1e-6
K_MAX = 1.0 - 1e-6
_SPLIT_SIZES = (E_CONV, E_CONV, E_CONV,
                E_FOURIER, E_FOURIER,
                E_REC, E_REC, E_REC, E_REC, E_REC,
                N_BRANCH * D_MODEL)
D_IN = 3 * E_CONV + 2 * E_FOURIER + 5 * E_REC + N_BRANCH * D_MODEL

kernel_name = "hybrid_conv_fourier_hgrn2_dit_block"

def _rmsnorm(x, g):
    x32 = x.astype(jnp.float32)
    y = x32 * lax.rsqrt(jnp.mean(x32 * x32, axis=-1, keepdims=True) + EPS)
    return (y * g.astype(jnp.float32)).astype(x.dtype)

def _layernorm(x, g, b):
    x32 = x.astype(jnp.float32)
    mu = jnp.mean(x32, axis=-1, keepdims=True)
    xc = x32 - mu
    y = xc * lax.rsqrt(jnp.mean(xc * xc, axis=-1, keepdims=True) + EPS)
    return (y * g.astype(jnp.float32) + b.astype(jnp.float32)).astype(x.dtype)

def _sincos_2d(rows, cols, d):
    quarter = d // 4
    omega = 1.0 / (10000.0 ** (jnp.arange(quarter, dtype=jnp.float32) / quarter))
    er = jnp.arange(rows, dtype=jnp.float32)[:, None] * omega
    ec = jnp.arange(cols, dtype=jnp.float32)[:, None] * omega
    emb_r = jnp.concatenate([jnp.sin(er), jnp.cos(er)], axis=-1)
    emb_c = jnp.concatenate([jnp.sin(ec), jnp.cos(ec)], axis=-1)
    emb = jnp.concatenate([jnp.broadcast_to(emb_r[:, None, :], (rows, cols, d // 2)),
                           jnp.broadcast_to(emb_c[None, :, :], (rows, cols, d // 2))], axis=-1)
    return emb.reshape(rows * cols, d)

def _split_proj(p):
    out, idx = [], 0
    for s in _SPLIT_SIZES:
        out.append(p[..., idx:idx + s])
        idx += s
    return out

def _depthwise(u, w):
    pad = CONV_WIDTH // 2
    return lax.conv_general_dilated(u, w.astype(u.dtype), window_strides=(1,), padding=[(pad, pad)],
                                    dimension_numbers=('NWC', 'WIO', 'NWC'),
                                    feature_group_count=u.shape[-1])

def _fourier(u):
    b, t, e = u.shape
    ug = u.astype(jnp.float32).reshape(b, t, FOURIER_GROUPS, e // FOURIER_GROUPS)
    f = jnp.fft.fft2(ug, axes=(1, 3), norm="ortho").real
    return f.reshape(b, t, e).astype(u.dtype)

def _rec_inputs(q, f_logit, i, lb):
    b, t, _ = q.shape
    z = f_logit.astype(jnp.float32)
    k = jnp.minimum((1.0 - lb) * jax.nn.sigmoid(-z), K_MAX)
    logf = jnp.log1p(-k)
    shp = (b, t, REC_HEADS, REC_KEY)
    return (q.astype(jnp.float32).reshape(shp), k.reshape(shp),
            i.astype(jnp.float32).reshape(b, t, REC_HEADS, REC_VAL), logf.reshape(shp))

def _chunks(a):
    b, t, h, d = a.shape
    return a.reshape(b, t // CHUNK, CHUNK, h, d).transpose(1, 0, 3, 2, 4)

def _unchunk(a):
    n, b, h, l, d = a.shape
    return a.transpose(1, 0, 3, 2, 4).reshape(b, n * l, h, d)

def _chunk_scan(q, k, v, logf, s0):
    mask = jnp.tril(jnp.ones((CHUNK, CHUNK), dtype=bool))[:, :, None]

    def step(S, inp):
        qc, kc, vc, gc = inp
        bcum = jnp.cumsum(gc, axis=2)
        b_last = bcum[:, :, -1:, :]
        o_inter = jnp.einsum('bhlk,bhkv->bhlv', qc * jnp.exp(bcum), S)
        diff = bcum[:, :, :, None, :] - bcum[:, :, None, :, :]
        decay = jnp.where(mask, jnp.exp(jnp.where(mask, diff, 0.0)), 0.0)
        scores = jnp.einsum('bhtk,bhsk,bhtsk->bhts', qc, kc, decay)
        o_intra = jnp.einsum('bhts,bhsv->bhtv', scores, vc)
        k_dec = kc * jnp.exp(b_last - bcum)
        S_new = jnp.exp(b_last[:, :, 0, :, None]) * S + jnp.einsum('bhlk,bhlv->bhkv', k_dec, vc)
        return S_new, o_inter + o_intra

    s_fin, o = lax.scan(step, s0, (_chunks(q), _chunks(k), _chunks(v), _chunks(logf)))
    return _unchunk(o), s_fin

def _flip(a):
    return a[:, ::-1]

def _mix(parts, o_rec, conv_w, conv_b, ln_g, ln_b, rec_g, w_pa, w_pb, w_pc, w_out):
    a_val, a_gate, a_z, b_u, b_z, _q, _ff, _fb, _i, c_z, gates = parts
    u = a_val * jax.nn.sigmoid(a_gate)
    u = _depthwise(u, conv_w) + conv_b
    u = _layernorm(u, ln_g, ln_b)
    y_a = (jax.nn.silu(u) * jax.nn.silu(a_z)) @ w_pa
    y_b = (_fourier(b_u) * jax.nn.silu(b_z)) @ w_pb
    bsz, t = o_rec.shape[0], o_rec.shape[1]
    o = o_rec * lax.rsqrt(jnp.mean(o_rec * o_rec, axis=-1, keepdims=True) + EPS)
    o = (o.reshape(bsz, t, E_REC) * rec_g.astype(jnp.float32)).astype(c_z.dtype)
    y_c = (o * jax.nn.silu(c_z)) @ w_pc
    g_a, g_b, g_c = jnp.split(jax.nn.sigmoid(gates), N_BRANCH, axis=-1)
    y = g_a * y_a + g_b * y_b + g_c * y_c
    return y @ w_out

def setup_inputs(seed: int = 0) -> dict:
    key = jax.random.key(seed)
    ks = jax.random.split(key, 24)

    def nrm(k, shape, scale):
        return jax.random.normal(k, shape, jnp.float32) * scale

    return {
        "x": nrm(ks[0], (BATCH, SEQ, D_MODEL), 1.0),
        "c": nrm(ks[1], (BATCH, D_MODEL), 1.0),
        "ctx": nrm(ks[2], (BATCH, CTX_LEN, D_MODEL), 1.0),
        "c_ctx": nrm(ks[3], (D_MODEL,), 1.0),
        "w_ada": nrm(ks[4], (DEPTH, D_MODEL, 3 * D_MODEL), 0.5 * D_MODEL ** -0.5),
        "b_ada": nrm(ks[5], (DEPTH, 3 * D_MODEL), 0.02),
        "norm_g": 1.0 + nrm(ks[6], (DEPTH, D_MODEL), 0.02),
        "w_in": nrm(ks[7], (DEPTH, D_MODEL, D_IN), D_MODEL ** -0.5),
        "conv_w": nrm(ks[8], (DEPTH, CONV_WIDTH, 1, E_CONV), CONV_WIDTH ** -0.5),
        "conv_b": nrm(ks[9], (DEPTH, E_CONV), 0.02),
        "conv_ln_g": 1.0 + nrm(ks[10], (DEPTH, E_CONV), 0.02),
        "conv_ln_b": nrm(ks[11], (DEPTH, E_CONV), 0.02),
        "rec_lb": nrm(ks[12], (2, DEPTH, E_REC), 0.5),
        "rec_norm_g": 1.0 + nrm(ks[13], (DEPTH, E_REC), 0.02),
        "w_pa": nrm(ks[14], (DEPTH, E_CONV, D_MODEL), E_CONV ** -0.5),
        "w_pb": nrm(ks[15], (DEPTH, E_FOURIER, D_MODEL), E_FOURIER ** -0.5),
        "w_pc": nrm(ks[16], (DEPTH, E_REC, D_MODEL), E_REC ** -0.5),
        "w_out": nrm(ks[17], (DEPTH, D_MODEL, D_MODEL), D_MODEL ** -0.5),
        "final_g": 1.0 + nrm(ks[18], (D_MODEL,), 0.02),
    }

def reference(x, c, ctx, c_ctx, w_ada, b_ada, norm_g, w_in, conv_w, conv_b, conv_ln_g, conv_ln_b,
              rec_lb, rec_norm_g, w_pa, w_pb, w_pc, w_out, final_g):
    n_tok = x.shape[1]
    rows = n_tok // GRID_W
    x = x + _sincos_2d(rows, GRID_W, D_MODEL).astype(x.dtype)[None]
    lb_soft = jax.nn.softmax(rec_lb.astype(jnp.float32), axis=1)
    lbs = jnp.cumsum(lb_soft, axis=1) - lb_soft[:, :1]
    bsz = x.shape[0]
    s_zero = jnp.zeros((bsz, REC_HEADS, REC_KEY, REC_VAL), jnp.float32)

    for l in range(DEPTH):
        last = l == DEPTH - 1
        shift_x, scale_x, gate_x = jnp.split(jax.nn.silu(c) @ w_ada[l] + b_ada[l], 3, axis=-1)
        shift_c, scale_c, gate_c = jnp.split(jax.nn.silu(c_ctx) @ w_ada[l] + b_ada[l], 3, axis=-1)
        hx = _rmsnorm(x, norm_g[l]) * (1.0 + scale_x[:, None]) + shift_x[:, None]
        hc = _rmsnorm(ctx, norm_g[l]) * (1.0 + scale_c) + shift_c
        px = _split_proj(hx @ w_in[l])
        pc = _split_proj(hc @ w_in[l])

        lb_f, lb_b = lbs[0, l], lbs[1, l]
        qc_, kcf, vc_, lcf = _rec_inputs(pc[5], pc[6], pc[8], lb_f)
        _, kcb, _, lcb = _rec_inputs(pc[5], pc[7], pc[8], lb_b)
        qx_, kxf, vx_, lxf = _rec_inputs(px[5], px[6], px[8], lb_f)
        _, kxb, _, lxb = _rec_inputs(px[5], px[7], px[8], lb_b)

        o_cf, s_cf = _chunk_scan(qc_, kcf, vc_, lcf, s_zero)
        o_cb, s_cb = _chunk_scan(_flip(qc_), _flip(kcb), _flip(vc_), _flip(lcb), s_zero)
        o_xf, _ = _chunk_scan(qx_, kxf, vx_, lxf, s_cf)
        o_xb, _ = _chunk_scan(_flip(qx_), _flip(kxb), _flip(vx_), _flip(lxb), s_cb)
        o_x = o_xf + _flip(o_xb)

        y_x = _mix(px, o_x, conv_w[l], conv_b[l], conv_ln_g[l], conv_ln_b[l], rec_norm_g[l],
                   w_pa[l], w_pb[l], w_pc[l], w_out[l])
        x = x + gate_x[:, None] * y_x
        if not last:
            o_c = o_cf + _flip(o_cb)
            y_c = _mix(pc, o_c, conv_w[l], conv_b[l], conv_ln_g[l], conv_ln_b[l], rec_norm_g[l],
                       w_pa[l], w_pb[l], w_pc[l], w_out[l])
            ctx = ctx + gate_c * y_c

    return _rmsnorm(x, final_g)


_drawn_inputs = setup_inputs


def setup_inputs(seed=0):
    import zlib

    import numpy as np

    out = dict(_drawn_inputs(seed))
    spreads = {}
    factors = {'ctx': 8.0,
     'c_ctx': 8.0,
     'b_ada': 3.797,
     'norm_g': 7.487,
     'conv_b': 8.0,
     'conv_ln_g': 21.452,
     'conv_ln_b': 23.277,
     'rec_lb': 2.737,
     'rec_norm_g': 8.0,
     'final_g': 8.497}
    for name, (base, spread) in spreads.items():
        noise = np.random.default_rng([zlib.crc32(name.encode()), seed]).standard_normal(out[name].shape)
        drawn = base * np.exp(spread * noise) if base else spread * noise
        out[name] = __import__('jax').numpy.asarray(drawn.astype(out[name].dtype))
    for name, factor in factors.items():
        out[name] = (out[name] * factor).astype(out[name].dtype)
    return out
```

```python
from contextlib import ExitStack

import numpy as np

import concourse.bass as bass
from concourse import mybir

P = 128
D_MODEL = 1024
DEPTH = 2
NX = 512
NCTX = 256
T_ALL = NX + NCTX
GRID_W = 64
E_CONV = 768
E_FOURIER = 512
E_REC = 768
TAPS = 31
PAD = TAPS // 2
EPS = 1e-6
K_MAX = 1.0 - 1e-6

KD = D_MODEL // P
JC = E_CONV // P
GF = E_FOURIER // P
HR = E_REC // P
CHUNK = 128
SUB = 32
LEVELS = [0, 1, 2, 4, 8, 16, 32, 64]
NLEV = len(LEVELS)
NMASK = 6
NMIX = 5
ADA_W = 512

F32 = mybir.dt.float32
F32R = mybir.dt.float32r
I32 = mybir.dt.int32
ALU = mybir.AluOpType
ACT = mybir.ActivationFunctionType

VPL = 242
V_NORM, V_BADA, V_CW, V_CB, V_LG, V_LB, V_RG = 0, 8, 32, 218, 224, 230, 236
V_RLB = DEPTH * VPL
V_FG = V_RLB + 24
V_CC = V_FG + KD
NVEC = V_CC + 2 * KD

D_XC, D_XS = 0, 4 * NX
D_CC, D_CS = 8 * NX, 8 * NX + 2 * NCTX
D_CH = 8 * NX + 4 * NCTX
NPOS = KD // 2 * (NX // GRID_W + GRID_W)
NDFT = D_CH + 2 * P

K_ID, K_SEL, K_MSK, K_ASEL = 0, P, 7 * P, 7 * P + SUB
NCONST = 7 * P + SUB + 4

N_B, N_PB, N_R, N_CZ, N_C, N_PC, N_PA, N_O = 2 * GF, 2 * KD, 4 * HR, HR, 5 * JC, 2 * (KD - JC), 2 * KD, KD
U_B = 0
U_PB = U_B + N_B
U_R = U_PB + N_PB
U_CZ = U_R + N_R
U_C = U_CZ + N_CZ
U_PC = U_C + N_C
U_PA = U_PC + N_PC
U_O = U_PA + N_PA
N_UNITS = U_O + N_O
KB, KC_, KA = E_FOURIER // P, E_REC // P, E_CONV // P


def build(nc, x_in, pos_in, vec_in, const_in, mask_in, dft_in, w_b, w_r, w_cz, w_c, w_g, w_pa, w_pb, w_pc, w_o, w_ada, out):
    ctx = ExitStack()
    with ctx:
        def sb(name, shape, dt=F32):
            return ctx.enter_context(nc.sbuf_tensor(name, shape, dt))

        def sem(name):
            return ctx.enter_context(nc.semaphore(name))

        hh = sb("hh", [P, KD, T_ALL], F32R)
        hl = sb("hl", [P, KD, T_ALL], F32R)
        raw = sb("raw", [P, 2, 1024])
        whi = sb("whi", [P, 2, 1024], F32R)
        wlo = sb("wlo", [P, 2, 1024], F32R)
        vec = sb("vec", [P, NVEC])
        const = sb("const", [P, NCONST])
        masks = sb("masks", [P, NMASK, SUB], I32)
        onecol = sb("onecol", [P, 64])
        cstat = sb("cstat", [P, KD, 32])
        ctmp = sb("ctmp", [P, 2 * KD])
        adat = sb("adat", [P, 24, 2])
        coef = sb("coef", [P, KD, 2])
        oml = sb("oml", [P, DEPTH, 2, HR])
        lbw = sb("lbw", [P, 8, 12])
        wj = sb("wj", [P, 32])
        sta = sb("sta", [P, 192])
        stb = sb("stb", [P, 192])
        stc = sb("stc", [P, 192])

        WORK_KB = 122
        w0 = nc.sbuf_base
        w0 = (w0 + 31) // 32 * 32
        ctx.enter_context(nc.sbuf_tensor("work_area", [P, WORK_KB * 256 + 8], F32))

        def at(name, kb, shape, dt=F32):
            t = nc.alloc_sbuf_tensor_at(name, shape, dt, offset=w0 + int(kb * 1024))
            assert int(kb * 1024) + int(np.prod(shape[1:])) * 4 <= WORK_KB * 1024, name
            return t

        y = at("y", 0, [P, KD, T_ALL])
        pos = at("pos", 0, [P, NPOS])
        sq_h = at("sq_h", 16, [P, 2, T_ALL])
        dft_raw = at("dft_raw", 0, [P, NDFT])
        bt = at("bt", 21, [P, T_ALL])
        x = at("x", 24, [P, KD, T_ALL])
        abh = at("abh", 24, [P, GF, T_ALL], F32R)
        abl = at("abl", 36, [P, GF, T_ALL], F32R)
        dch = at("dch", 48, [P, NDFT], F32R)
        dcl = at("dcl", 69, [P, NDFT], F32R)
        ada_w = [at("ada_w_shift", 56, [P, 2, KD, ADA_W]), at("ada_w_scale", 88, [P, 2, KD, ADA_W]),
                 at("ada_w_gate", 60, [P, 2, KD, ADA_W])]
        ada_row = at("ada_row", 120, [P, ADA_W])
        ht = at("ht", 88, [P, 2, T_ALL])
        hf = at("hf", 94, [P, 2, T_ALL])
        bz = at("bz", 90, [P, T_ALL])
        bur = at("bur", 93, [P, T_ALL])
        buh = at("buh", 96, [P, T_ALL], F32R)
        bul = at("bul", 99, [P, T_ALL], F32R)
        ar = at("ar", 102, [P, 6 * 2 * P])
        ahi = at("ahi", 108, [P, 6 * 2 * P], F32R)
        alo = at("alo", 114, [P, 6 * 2 * P], F32R)
        sig = at("sig", 24, [P, 2, T_ALL])
        stq = at("stq", 30, [P, T_ALL])
        stv = at("stv", 33, [P, T_ALL])
        ff = at("ff", 36, [P, 2, T_ALL])
        qq = at("qq", 42, [P, 2, T_ALL])
        kk = at("kk", 48, [P, 2, T_ALL])
        ks = at("ks", 54, [P, T_ALL])
        tl = {1: ff}
        off = 57.0
        for m in (2, 4, 8, 16, 32, 64, 128):
            tl[m] = at(f"tl{m}", off, [P, 2, T_ALL // m])
            off += 2 * T_ALL / m * 4 / 1024
        near = at("near", 63, [P, 6 * SUB])
        sc = at("sc", 64, [P, 6, CHUNK])
        vt = at("vt", 67, [P, 6, P])
        kt = at("kt", 70, [P, 2, 5, P])
        st = at("st", 75, [P, 2, 5, P])
        ot = at("ot", 80, [P, HR, T_ALL])
        km = at("km", 116, [P, 2, T_ALL])
        cz = at("cz", 98, [P, HR, T_ALL])
        ach = at("ach", 24, [P, JC, T_ALL], F32R)
        acl = at("acl", 42, [P, JC, T_ALL], F32R)
        sq_r = at("sq_r", 60, [P, 2, T_ALL])
        t1 = at("t1", 66, [P, 2, T_ALL])
        az = at("az", 60, [P, JC, T_ALL])
        cu = at("cu", 78, [P, JC, T_ALL])
        UBW = T_ALL + 4 * PAD
        ub = at("ub", 96, [P, UBW])
        acca = at("acca", 99.5, [P, UBW - 2 * PAD])
        accb = at("accb", 103, [P, UBW - 2 * PAD])
        sg = at("sg", 116, [P, T_ALL])
        av = at("av", 119, [P, T_ALL])
        sq_l = at("sq_l", 96, [P, 2, T_ALL])
        lu = at("lu", 102, [P, 2, T_ALL])
        tm = at("tm", 114, [P, 2, T_ALL])
        gst = at("gst", 108, [P, T_ALL])
        pst = at("pst", 111, [P, T_ALL])
        gst_b = at("gst_b", 102, [P, T_ALL])
        pst_b = at("pst_b", 105, [P, T_ALL])
        oxs = at("oxs", 48, [P, 2, T_ALL])
        outb = at("outb", 48, [P, KD, NX])

        ident = const[:, K_ID:K_ID + P]
        asel = const[:, K_ASEL:K_ASEL + 4]

        ps = [ctx.enter_context(nc.psum_tensor(f"unit{k}", [P, 1024], F32)) for k in range(2)]
        aux = ctx.enter_context(nc.psum_tensor("aux", [P, 2048], F32))
        x_keep = nc.dram_tensor("x_keep", [P, KD, T_ALL], F32, kind="Internal").ap()

        raw_full = [sem("raw_full0"), sem("raw_full1")]
        vec_in_s, const_s, mask_s, x_s, pos_s, dft_s = [sem(n) for n in ("vec_loaded", "const_loaded", "masks_loaded", "x_loaded", "pos_loaded", "dft_loaded")]
        ada_full = [sem("ada_shift_loaded"), sem("ada_scale_loaded"), sem("ada_gate_loaded")]
        x_kept, x_back, out_s = sem("x_kept"), sem("x_back"), sem("out_stored")
        split, rounded = sem("unit_split"), sem("weights_rounded")
        unit_mm, unit_out = sem("unit_multiplied"), sem("unit_taken_out")
        setup, c_ready, lb_e, lb_r = sem("setup"), sem("c_sigmoid"), sem("lb_exp"), sem("c_silu_ready")
        x_ready, h_ready = sem("x_ready"), sem("h_ready")
        ada_mm, ada_rowed, ada_tmm, ada_t = sem("ada_rows_multiplied"), sem("ada_rows_out"), sem("ada_columns_multiplied"), sem("ada_ready")
        sq_ready, sq_used = sem("squares_ready"), sem("squares_summed")
        stat_mm, stat_v, stat_s, stat_r = sem("mean_summed"), sem("variance_ready"), sem("root_ready"), sem("scale_ready")
        bc_mm, bc_used = sem("scale_spread"), sem("spread_used")
        ht_ready, hf_ready = sem("normed_ready"), sem("modulated_ready")
        dft_h, dft_ready = sem("dft_rounded"), sem("dft_split")
        bulo, dft1_mm, a_out, alo_s = sem("bu_split"), sem("dft1_done"), sem("dft1_out"), sem("dft1_split")
        dft2_mm, abt, abh_s, abl_s = sem("dft2_done"), sem("fourier_gated"), sem("fourier_rounded"), sem("fourier_split")
        p_done, y_ready = sem("merge_done"), sem("y_split")
        v_tr, vt_s, lvl_mm, k_ready, q_ready, lvl_used = sem("v_transposed"), sem("v_rows_ready"), sem("level_multiplied"), sem("level_k_ready"), sem("level_q_ready"), sem("level_taken_out")
        k_tr, kt_s, ds_mm, s_ready, o_mm, o_out, sc_s, km_s = sem("k_transposed"), sem("k_rows_ready"), sem("state_terms_ready"), sem("states_ready"), sem("o_multiplied"), sem("o_out"), sem("scores_ready"), sem("k_mixed")
        tm_s, ac_h, ac_l, ca_l = sem("operand_ready"), sem("operand_rounded"), sem("rec_operand_split"), sem("conv_operand_split")
        u_done, conv_done = sem("conv_input_ready"), sem("conv_done")
        xc_s, lnt_s, lu_s = sem("centred"), sem("ln_scaled"), sem("ln_silu_ready")
        passed = {n: sem(f"{n}_passed") for n in ("act", "dve", "pool")}
        dve_done, act_done = sem("dve_done"), sem("act_done")
        y_out = sem("output_ready")

        def rows(t, off_, *dims, p0=0, n=P):
            width = int(np.prod(t.shape[1:]))
            return bass.AP(t, p0 * width + off_, [[width, n], *[list(d) for d in dims]])

        def wait(e, s, v):
            if not (isinstance(v, int) and v <= 0):
                e.wait_ge(s, v)

        class Done:
            def __init__(self, e, s):
                self.e, self.s, self.base, self.n, self.signals = e, s, 0, 0, []

            def add(self, ins, s=None, v=None):
                if s is None:
                    self.n += 1
                    s, v = self.s, self.base + self.n
                self.signals.append((s, v))
                return ins.then_inc(s, 1)

            def all_but(self, lag=0):
                s, v = self.signals[-1 - lag]
                assert v is not None
                wait(self.e, s, v)

            def start(self, base):
                self.base, self.n, self.signals = base, 0, [(self.s, base), (self.s, base)]

        def tokens(l):
            return T_ALL if l == 0 else NX

        def halves(t):
            return [(0, NX), (NX, T_ALL)] if t == T_ALL else [(0, NX)]

        def segs(t):
            return [(0, 0, NX), (1, NX, T_ALL)] if t == T_ALL else [(0, 0, NX)]

        def half0(l, u):
            return (l * N_UNITS + u) // 2

        class Unit:
            def __init__(self, half, k=0):
                self.half, self.slot = half + k // 2, k % 2
                self.n = self.half * 2 + self.slot

        def chunks(l):
            return tokens(l) // CHUNK
        FWD, BWD = [4, 5, 0, 1, 2], [5, 4, 3, 2, 1]

        SQN = [8, 6, 0, 6, 8, 6, 0, 6, 8]
        BCN = [1, 6, 1, 1, 1, 6, 1, 1, 1]
        sq0 = [sum(SQN[:i]) for i in range(10)]
        bc0 = [sum(BCN[:i]) for i in range(10)]

        def fresh(i):
            return sum(1 for k in range(i) if k not in (2, 6))

        def quarters(ap2, w):
            return ap2.rearrange("p (j w) -> p j w", w=w)

        def spread(w):
            return aux[:, :].rearrange("p (b c) -> p b c", b=4)[:, :, 0:w]

        block = ctx.enter_context(nc.Block())

        @block.sync
        def _(sp):
            def load(u, src, first=False):
                n = src.shape[-1]
                if not first:
                    wait(sp, split, u.n - 1)
                sp.dma_start(raw[:, u.slot, 0:n], src).then_inc(raw_full[u.slot], 16)

            sp.dma_start(vec[:, :], vec_in).then_inc(vec_in_s, 16)
            sp.dma_start(const[:, :], const_in).then_inc(const_s, 16)
            sp.dma_start(x[:, :, :], x_in).then_inc(x_s, 16)
            sp.dma_start(pos[:, :], pos_in).then_inc(pos_s, 16)
            sp.dma_start(ada_w[0][:, :, :, :], w_ada[0, 0]).then_inc(ada_full[0], 16)
            sp.dma_start(ada_w[1][:, :, :, :], w_ada[0, 1]).then_inc(ada_full[1], 16)
            sp.dma_start(masks[:, :, :], mask_in).then_inc(mask_s, 16)
            for l in range(DEPTH):
                if l == 0:
                    for k in range(2):
                        load(Unit(0, k), w_b[0, k], first=True)
                with sp.Fori(1 if l == 0 else 0, GF) as g:
                    for k in range(2):
                        load(Unit(half0(l, U_B) + g, k), w_b[l, g * 2 + k])
                with sp.Fori(0, KD) as d:
                    load(Unit(half0(l, U_PB) + d, 0), w_g[l, 1, d])
                    load(Unit(half0(l, U_PB) + d, 1), w_pb[l, d])
                with sp.Fori(0, HR) as h:
                    for k in range(4):
                        load(Unit(half0(l, U_R) + h * 2, k), w_r[l, h * 4 + k])
                with sp.Fori(0, HR // 2) as h:
                    for k in range(2):
                        load(Unit(half0(l, U_CZ) + h, k), w_cz[l, h * 2 + k])
                with sp.Fori(0, JC // 2) as m:
                    for s in range(2):
                        for k in range(3):
                            load(Unit(half0(l, U_C) + m * 5, 5 * s + k), w_c[l, m * 6 + (3 * s + k)])
                        load(Unit(half0(l, U_C) + m * 5, 5 * s + 3), w_g[l, 2, m * 2 + s])
                        load(Unit(half0(l, U_C) + m * 5, 5 * s + 4), w_pc[l, m * 2 + s])
                for d in range(JC, KD):
                    load(Unit(half0(l, U_PC) + d - JC, 0), w_g[l, 2, d])
                    load(Unit(half0(l, U_PC) + d - JC, 1), w_pc[l, d])
                with sp.Fori(0, KD) as d:
                    load(Unit(half0(l, U_PA) + d, 0), w_g[l, 0, d])
                    load(Unit(half0(l, U_PA) + d, 1), w_pa[l, d])
                with sp.Fori(0, KD // 2) as d:
                    for k in range(2):
                        load(Unit(half0(l, U_O) + d, k), w_o[l, d * 2 + k])

        @block.gpsimd
        def _(pool):
            def split_unit(u, n=1024):
                s = u.slot
                wait(pool, raw_full[s], u.half * 16 + 16)
                wait(pool, unit_mm, u.n - 1)
                pool.sem_inc(passed["pool"], 1)
                nc.gpsimd.tensor_scalar(whi[:, s, 0:n], raw[:, s, 0:n], 1.0, 0.0, ALU.mult, ALU.add).then_inc(rounded, 1)
                wait(pool, rounded, u.n + 1)
                nc.gpsimd.tensor_tensor(wlo[:, s, 0:n], raw[:, s, 0:n], whi[:, s, 0:n].bitcast(F32), ALU.subtract).then_inc(split, 1)

            for l in range(DEPTH):
                if l == 0:
                    for k in range(2):
                        split_unit(Unit(0, k))
                with pool.Fori(1 if l == 0 else 0, GF) as g:
                    for k in range(2):
                        split_unit(Unit(half0(l, U_B) + g, k))
                with pool.Fori(0, KD) as d:
                    split_unit(Unit(half0(l, U_PB) + d, 0))
                    split_unit(Unit(half0(l, U_PB) + d, 1), KB * P)
                with pool.Fori(0, (4 * HR + HR) // 2) as h:
                    for k in range(2):
                        split_unit(Unit(half0(l, U_R) + h, k))
                with pool.Fori(0, JC // 2) as m:
                    for s in range(2):
                        for k in range(4):
                            split_unit(Unit(half0(l, U_C) + m * 5, 5 * s + k))
                        split_unit(Unit(half0(l, U_C) + m * 5, 5 * s + 4), KC_ * P)
                with pool.Fori(0, KD - JC) as d:
                    split_unit(Unit(half0(l, U_PC) + d, 0))
                    split_unit(Unit(half0(l, U_PC) + d, 1), KC_ * P)
                split_unit(Unit(half0(l, U_PA), 0))
                split_unit(Unit(half0(l, U_PA), 1), KA * P)
                for k in range(JC):
                    pool.wait_ge(ac_h, (2 * l + 1) * HR + k + 1)
                    t = tokens(l)
                    nc.gpsimd.tensor_tensor(acl[:, k, 0:t], tm[:, k % 2, 0:t], ach[:, k, 0:t].bitcast(F32), ALU.subtract).then_inc(ca_l, 1)
                with pool.Fori(1, KD) as d:
                    split_unit(Unit(half0(l, U_PA) + d, 0))
                    split_unit(Unit(half0(l, U_PA) + d, 1), KA * P)
                with pool.Fori(0, KD // 2) as d:
                    for k in range(2):
                        split_unit(Unit(half0(l, U_O) + d, k))

        @block.tensor
        def _(pe):
            def begin(u):
                wait(pe, split, u.n + 1)
                wait(pe, unit_out, u.n - 1)

            def part(u, t, kcs, nk=KD, rh=hh, rl=hl, ready=None):
                ins = None
                for kc in kcs:
                    if ready is not None:
                        wait(pe, ready[0], ready[1] + kc + 1)
                    for n, (a, b) in enumerate(((whi, rh), (whi, rl), (wlo, rh))):
                        for (c0, c1) in halves(t):
                            ins = nc.tensor.matmul(ps[u.slot][:, c0:c1], a[:, u.slot, kc * P:(kc + 1) * P], b[:, kc, c0:c1],
                                                   start=(kc == 0 and n == 0), stop=(kc == nk - 1 and n == 2))
                if nk - 1 in kcs:
                    ins.then_inc(unit_mm, 1)

            def unit(u, t, nk=KD, rh=hh, rl=hl, ready=None):
                begin(u)
                part(u, t, range(nk), nk, rh, rl, ready)

            def ada(l, b):
                n = 3 * l + b
                wait(pe, ada_full[b], 16 * (l + 1))
                if n == 0:
                    pe.wait_ge(setup, 1)
                    pe.wait_ge(lb_r, 1)
                wait(pe, ada_t, n)
                for k4 in range(KD // 2):
                    for q in range(4):
                        kc = (q % 2) * (KD // 2) + k4
                        ins = nc.tensor.matmul(aux[32 * q:32 * q + 32, 1536:2048], cstat[:, kc, :], ada_w[b][:, q // 2, kc, :],
                                               start=(k4 == 0), stop=(k4 == KD // 2 - 1))
                ins.then_inc(ada_mm, 1)
                pe.wait_ge(ada_rowed, n + 1)
                pe.wait_ge(const_s, 16)
                for b4 in range(4):
                    ins = nc.tensor.matmul(aux[:, 1536 + 4 * b4:1540 + 4 * b4], ada_row[:, b4 * P:(b4 + 1) * P], asel, start=True, stop=True)
                ins.then_inc(ada_tmm, 1)

            def sums(i, tiles, w, src, ready, col_of=lambda k: 0, squares=True):
                wait(pe, bc_used, bc0[i])
                for k in range(tiles):
                    wait(pe, ready[0], ready[1] + k + 1)
                    c = col_of(k)
                    for j in range(4):
                        ins = nc.tensor.matmul(aux[32 * j:32 * j + 32, 0:w], onecol[:, 32 - c:64 - c], src(k)[:, j * w:(j + 1) * w],
                                               start=(k == 0), stop=(k == tiles - 1))
                    if squares:
                        ins.then_inc(sq_used, 1)
                if not squares:
                    ins.then_inc(stat_mm, 1)

            def spread_rows(i, r, w, src, ready):
                wait(pe, ready[0], ready[1])
                wait(pe, bc_used, bc0[i] + r)
                for j in range(4):
                    ins = nc.tensor.matmul(aux[:, 512 * j:512 * j + w], const[32 * j:32 * j + 32, K_SEL + r * P:K_SEL + (r + 1) * P],
                                           src[32 * j:32 * j + 32, 0:w], start=True, stop=True)
                ins.then_inc(bc_mm, 1)

            def x_sums(i, w, first, n=2, stop=False):
                wait(pe, sq_ready, first + sq0[i] + n)
                for k in range(n):
                    for j in range(4):
                        ins = nc.tensor.matmul(aux[32 * j:32 * j + 32, 0:w], onecol[:, 32:64], sq_h[:, k % 2, j * w:(j + 1) * w],
                                               start=False, stop=stop and k == n - 1)
                    ins.then_inc(sq_used, 1)

            def clear_sums(i, w):
                wait(pe, bc_used, bc0[i])
                for j in range(4):
                    nc.tensor.matmul(aux[32 * j:32 * j + 32, 0:w], onecol[:, 0:32], const[:, 0:w], start=True, stop=False)

            def dft1(l, g):
                G = l * GF + g
                wait(pe, unit_out, Unit(half0(l, U_B) + g, 0).n + 1)
                wait(pe, bulo, G + 1)
                wait(pe, abt, G)
                pe.wait_ge(dft_ready, l + 1)
                for c in range(chunks(l)):
                    for n, (a, b) in enumerate(((buh, dch), (buh, dcl), (bul, dch))):
                        ins = nc.tensor.matmul(aux[:, 256 * c:256 * c + 256], a[:, c * P:(c + 1) * P], b[:, D_CH:D_CH + 2 * P], start=(n == 0), stop=(n == 2))
                ins.then_inc(dft1_mm, 1)

            def dft2(l, g):
                G = l * GF + g
                wait(pe, alo_s, G + 1)
                for (o, n, first, cnt, dc, ds) in ((1024, NX, 0, 4, D_XC, D_XS), (1536, NCTX, 4, 2, D_CC, D_CS)):
                    if first >= chunks(l):
                        continue
                    steps = [(c, p, q) for c in range(cnt) for p in range(2) for q in range(3)]
                    for (c, p, q) in steps:
                        a = (ahi, ahi, alo)[q]
                        b = (dch, dcl, dch)[q]
                        b0 = (dc, ds)[p] + c * n
                        a0 = (first + c) * 256 + p * P
                        ins = nc.tensor.matmul(aux[:, o:o + n], a[:, a0:a0 + P], b[:, b0:b0 + n],
                                               start=((c, p, q) == steps[0]), stop=((c, p, q) == steps[-1]))
                ins.then_inc(dft2_mm, 1)

            def recurrence(l, h, us):
                t = tokens(l)
                nch = chunks(l)
                H = h + l * HR
                A, B = 0, 1024

                def level(n):
                    m = LEVELS[n]
                    o = B if n % 2 == 0 else A
                    if n > 0:
                        wait(pe, q_ready, H * NLEV + n)
                    if n == 0 or m >= 32:
                        wait(pe, k_ready, H * NLEV + max(n, 1))
                    else:
                        wait(pe, km_s, H * NMIX + n)
                    if n == 0:
                        wait(pe, o_out, H)
                    elif n == 1:
                        wait(pe, vt_s, H + 1)
                    else:
                        wait(pe, lvl_used, H * (NLEV - 1) + n - 1)
                    for c in range(nch):
                        if m < 64:
                            for q in range(4):
                                tb = c * CHUNK + q * SUB
                                dst = aux[32 * q:32 * q + 32, o + c * SUB:o + (c + 1) * SUB]
                                if m == 0:
                                    a, b = ks[:, tb:tb + SUB], stq[:, tb:tb + SUB]
                                elif m < 32:
                                    a = km[:, n % 2, tb:tb + SUB]
                                    b = rows(qq, T_ALL + tb, [2 * m, SUB // (2 * m)], [m - T_ALL, 2], [1, m])
                                elif q % 2 == 0:
                                    a, b = kk[:, 0, tb:tb + SUB], qq[:, 0, tb + SUB:tb + 2 * SUB]
                                else:
                                    a, b = kk[:, 1, tb:tb + SUB], qq[:, 1, tb - SUB:tb]
                                ins = nc.tensor.matmul(dst, a, b, start=True, stop=True)
                        else:
                            c0 = c * CHUNK
                            nc.tensor.matmul(aux[0:64, o + c * 64:o + (c + 1) * 64], kk[:, 0, c0:c0 + 64], qq[:, 0, c0 + 64:c0 + 128], start=True, stop=True)
                            ins = nc.tensor.matmul(aux[64:128, o + c * 64:o + (c + 1) * 64], kk[:, 1, c0 + 64:c0 + 128], qq[:, 1, c0:c0 + 64], start=True, stop=True)
                    ins.then_inc(lvl_mm, 1)

                todo = [(u, tt, kc) for (u, tt) in us for kc in range(KD)]

                def fill(n):
                    for _ in range(min(n, len(todo))):
                        u, tt, kc = todo.pop(0)
                        if kc == 0:
                            begin(u)
                        part(u, tt, [kc])

                fill(3)
                wait(pe, unit_out, us[0][0].n)
                wait(pe, s_ready, 2 * H)
                for c in range(6):
                    ins = nc.tensor.transpose(aux[:, A + c * P:A + (c + 1) * P], stv[:, c * P:(c + 1) * P], ident)
                ins.then_inc(v_tr, 1)
                level(0)
                fill(1)
                level(1)
                for n in range(2, NLEV):
                    fill(3)
                    level(n)
                fill(3)
                for d, order, o in ((0, FWD, B), (1, BWD, A)):
                    wait(pe, k_ready, (H + 1) * NLEV)
                    if d == 0:
                        wait(pe, lvl_used, (H + 1) * (NLEV - 1))
                    else:
                        wait(pe, sc_s, H + 1)
                    for n, c in enumerate(order):
                        ins = nc.tensor.transpose(aux[:, o + n * P:o + (n + 1) * P], kk[:, d, c * P:(c + 1) * P], ident)
                    ins.then_inc(k_tr, 1)
                fill(3)
                for d, order, o in ((0, FWD, B), (1, BWD, A)):
                    wait(pe, kt_s, 2 * H + 1 + d)
                    for n, c in enumerate(order):
                        ins = nc.tensor.matmul(aux[:, o + n * P:o + (n + 1) * P], kt[:, d, n, :], vt[:, c, :], start=True, stop=True)
                    ins.then_inc(ds_mm, 1)
                fill(3)
                wait(pe, s_ready, 2 * H + 2)
                wait(pe, sc_s, H + 1)
                for c in range(nch):
                    terms = [(vt[:, c, :], sc[:, c, :])]
                    for d, order in ((0, FWD), (1, BWD)):
                        if c != order[0]:
                            n = order.index(c) - 1 if c in order else len(order) - 1
                            terms.append((st[:, d, n, :], qq[:, d, c * P:(c + 1) * P]))
                    for n, (a, b) in enumerate(terms):
                        ins = nc.tensor.matmul(aux[:, B + c * P:B + (c + 1) * P], a, b, start=(n == 0), stop=(n == len(terms) - 1))
                ins.then_inc(o_mm, 1)
                fill(len(todo))

            def merge(l, hb, nk, rh, rl, ready=None):
                t = tokens(l)
                unit(Unit(hb, 0), t)
                unit(Unit(hb, 1), t, nk, rh, rl, ready)

            for l in range(DEPTH):
                t = tokens(l)
                i0 = 4 * l
                if l == 0:
                    pe.wait_ge(setup, 1)
                    sums(0, KD, T_ALL // 4, lambda k: sq_h[:, k % 2, :], (sq_ready, 0))
                    ada(0, 0)
                    ada(0, 1)
                wait(pe, ada_t, 3 * l + 2)
                spread_rows(i0, 0, T_ALL // 4, stc, (stat_r, fresh(i0) + 1))
                first = [Unit(half0(l, U_B), k) for k in range(2)]
                for u in first:
                    begin(u)
                for kc in range(KD):
                    for u in first:
                        part(u, t, [kc], ready=(h_ready, l * KD))
                wait(pe, bc_used, bc0[i0] + 1)
                dft1(l, 0)
                with pe.Fori(1, GF) as g:
                    unit(Unit(half0(l, U_B) + g, 0), t)
                    dft2(l, g - 1)
                    unit(Unit(half0(l, U_B) + g, 1), t)
                    dft1(l, g)
                unit(Unit(half0(l, U_PB), 0), t)
                dft2(l, GF - 1)
                unit(Unit(half0(l, U_PB), 1), t, KB, abh, abl, ready=(abl_s, l * GF))
                with pe.Fori(1, KD) as d:
                    merge(l, half0(l, U_PB) + d, KB, abh, abl)
                wait(pe, abt, (l + 1) * GF)
                for k in range(4):
                    unit(Unit(half0(l, U_R), k), t if k == 2 else T_ALL)
                with pe.Fori(1, HR) as h:
                    recurrence(l, h - 1, [(Unit(half0(l, U_R) + h * 2, k), t if k == 2 else T_ALL) for k in range(4)])
                recurrence(l, HR - 1, [(Unit(half0(l, U_CZ), k), t) for k in range(4)])
                w = t // 4
                unit(Unit(half0(l, U_CZ), 4), t)
                wait(pe, o_out, (l + 1) * HR)
                sums(i0 + 1, HR, w, lambda k: sq_r[:, k % 2, :], (sq_ready, sq0[i0 + 1]), col_of=lambda k: k)
                u5 = Unit(half0(l, U_CZ), 5)
                begin(u5)
                part(u5, t, range(0, KD - HR))
                for r in range(HR):
                    spread_rows(i0 + 1, r, w, stc, (stat_r, fresh(i0 + 1) + 1))
                    part(u5, t, [KD - HR + r])
                with pe.Fori(0, JC // 2) as m:
                    for s in range(2):
                        for k in range(4):
                            unit(Unit(half0(l, U_C) + m * 5, 5 * s + k), t)
                        pe.wait_ge(ac_l, (l + 1) * HR)
                        unit(Unit(half0(l, U_C) + m * 5, 5 * s + 4), t, KC_, ach, acl)
                merge(l, half0(l, U_PC), KC_, ach, acl)
                sums(i0 + 2, JC, w, lambda k: cu[:, k, :], (conv_done, l * JC), squares=False)
                spread_rows(i0 + 2, 0, w, sta, (stat_v, i0 + 3))
                unit(Unit(half0(l, U_PC) + 1, 0), t)
                wait(pe, bc_used, bc0[i0 + 2] + 1)
                sums(i0 + 3, JC, w, lambda k: sq_l[:, k % 2, :], (sq_ready, sq0[i0 + 3]))
                unit(Unit(half0(l, U_PC) + 1, 1), t, KC_, ach, acl)
                spread_rows(i0 + 3, 0, w, stc, (stat_r, fresh(i0 + 3) + 1))
                unit(Unit(half0(l, U_PA), 0), t)
                unit(Unit(half0(l, U_PA), 1), t, KA, ach, acl, ready=(ca_l, l * JC))
                with pe.Fori(1, KD) as d:
                    merge(l, half0(l, U_PA) + d, KA, ach, acl)
                wait(pe, bc_used, bc0[i0 + 4])
                ada(l, 2)
                i, w = i0 + 4, t // 4
                unit(Unit(half0(l, U_O), 0), t, ready=(y_ready, l * KD))
                unit(Unit(half0(l, U_O), 1), t)
                clear_sums(i, w)
                with pe.Fori(1, KD // 2 - 1) as d:
                    for k in range(2):
                        unit(Unit(half0(l, U_O) + d, k), t)
                    x_sums(i, w, (d - 1) * 2)
                if l == 0:
                    ada(1, 0)
                    ada(1, 1)
                for k in range(2):
                    unit(Unit(half0(l, U_O) + KD // 2 - 1, k), t)
                x_sums(i, w, KD - 4)
                x_sums(i, w, KD - 2, n=1)
                wait(pe, sq_ready, sq0[i] + KD)
                for j in range(4):
                    ins = nc.tensor.matmul(aux[32 * j:32 * j + 32, 0:w], onecol[:, 32:64], sq_h[:, 1, j * w:(j + 1) * w], start=False, stop=True)
                ins.then_inc(sq_used, 1)
            spread_rows(8, 0, NX // 4, stc, (stat_r, fresh(8) + 1))

        @block.scalar
        def _(act):
            own = Done(act, act_done)

            def take(u, *ops):
                wait(act, unit_mm, u.n + 1)
                for n, op in enumerate(ops):
                    ins = op()
                    if n == len(ops) - 1:
                        ins.then_inc(unit_out, 1)

            def copy_to(dst, src, f=ACT.Copy, **kw):
                return lambda: nc.scalar.activation(dst, src, f, **kw)

            def held():
                act.sem_inc(passed["act"], 1)

            def ada(l, b):
                n = 3 * l + b
                act.wait_ge(ada_mm, n + 1)
                wait(act, ada_tmm, n)
                nc.scalar.activation(ada_row[:, :], aux[:, 1536:2048], ACT.Copy).then_inc(ada_rowed, 1)

            def squares(i, tiles, w4, dst, src, ready=None):
                for k in range(tiles):
                    if ready is not None:
                        wait(act, ready[0], ready[1] + k + 1)
                    wait(act, sq_used, sq0[i] + k - 1)
                    nc.scalar.activation(dst[:, k % 2, 0:w4], src(k), ACT.Square).then_inc(sq_ready, 1)

            def root(i, w):
                act.wait_ge(stat_v, i + 1)
                nc.scalar.activation(stb[:, 0:w], sta[:, 0:w], ACT.Sqrt).then_inc(stat_s, 1)

            def merge(l, hb, s, g_, p_):
                t = tokens(l)
                for k, (dst, f) in enumerate(((g_, ACT.Sigmoid), (p_, ACT.Copy))):
                    u = Unit(hb, k)
                    wait(act, p_done, s)
                    take(u, copy_to(dst[:, 0:t], ps[u.slot][:, 0:t], f))

            def operand(n0, k, t, dst_h):
                act.wait_ge(tm_s, n0 + k + 1)
                nc.scalar.activation(dst_h[:, k, 0:t], (t1 if (n0 // HR) % 2 == 0 else tm)[:, k % 2, 0:t], ACT.Copy).then_inc(ac_h, 1)

            act.wait_ge(setup, 2)
            own.add(nc.scalar.activation(lbw[:, 1, :], lbw[:, 1, :], ACT.Exp))
            own.add(nc.scalar.activation(lbw[:, 2, :], lbw[:, 2, :], ACT.Exp))
            own.all_but()
            nc.scalar.activation(ctmp[:, :], vec[:, V_CC:V_CC + 2 * KD], ACT.Sigmoid).then_inc(c_ready, 1)

            for l in range(DEPTH):
                t = tokens(l)
                i0 = 4 * l
                if l == 0:
                    squares(0, KD, T_ALL, sq_h, lambda k: x[:, k, :], ready=(x_ready, 0))
                root(i0, 192)
                if l == 0:
                    for b in range(2):
                        ada(0, b)
                act.wait_ge(sq_used, sq0[i0 + 1])
                act.wait_ge(ada_t, 3 * l + 2)
                act.dma_start(dft_raw[:, :], dft_in).then_inc(dft_s, 16)
                act.wait_ge(x_ready, (l + 1) * KD)
                act.dma_start(x_keep, x[:, :, :]).then_inc(x_kept, 16)
                for k in range(KD):
                    act.wait_ge(ht_ready, l * KD + k + 1)
                    wait(act, h_ready, l * KD + k - 1)
                    for (i, c0, c1) in segs(T_ALL):
                        own.add(nc.scalar.activation(hf[:, k % 2, c0:c1], ht[:, k % 2, c0:c1], ACT.Identity,
                                                     scale=coef[:, k, i:i + 1], bias=adat[:, k, i:i + 1]))
                    own.all_but()
                    nc.scalar.activation(hh[:, k, :], hf[:, k % 2, :], ACT.Copy).then_inc(hf_ready, 1)
                act.wait_ge(dft_s, 16 * (l + 1))
                act.wait_ge(h_ready, (l + 1) * KD)
                for n in range(4):
                    a, b = NDFT * n // 4, NDFT * (n + 1) // 4
                    nc.scalar.activation(dch[:, a:b], dft_raw[:, a:b], ACT.Copy).then_inc(dft_h, 1)

                def take_bu(g):
                    u = Unit(half0(l, U_B) + g, 0)
                    wait(act, bulo, l * GF + g)
                    wait(act, dft1_mm, l * GF + g)
                    take(u, copy_to(bur[:, 0:t], ps[u.slot][:, 0:t]), copy_to(buh[:, 0:t], ps[u.slot][:, 0:t]))

                def take_bz(g):
                    u = Unit(half0(l, U_B) + g, 1)
                    wait(act, abt, l * GF + g)
                    take(u, copy_to(bz[:, 0:t], ps[u.slot][:, 0:t], ACT.Silu))

                def take_dft1(g):
                    G = l * GF + g
                    n = 256 * chunks(l)
                    wait(act, dft1_mm, G + 1)
                    wait(act, alo_s, G)
                    wait(act, dft2_mm, G)
                    nc.scalar.activation(ar[:, 0:n], aux[:, 0:n], ACT.Copy)
                    nc.scalar.activation(ahi[:, 0:n], aux[:, 0:n], ACT.Copy).then_inc(a_out, 1)

                def round_fourier(g):
                    wait(act, abt, l * GF + g + 1)
                    if not isinstance(g, int):
                        held()
                    nc.scalar.activation(abh[:, g, 0:t], bt[:, 0:t], ACT.Copy).then_inc(abh_s, 1)

                take_bu(0)
                take_bz(0)
                take_dft1(0)
                act.wait_ge(x_kept, 16 * (l + 1))
                with act.Fori(1, GF) as g:
                    take_bu(g)
                    round_fourier(g - 1)
                    take_bz(g)
                    take_dft1(g)
                s0 = 24 * l
                act.wait_ge(alo_s, (l + 1) * GF)
                u = Unit(half0(l, U_PB), 0)
                take(u, copy_to(gst_b[:, 0:t], ps[0][:, 0:t], ACT.Sigmoid))
                round_fourier(GF - 1)
                u = Unit(half0(l, U_PB), 1)
                take(u, copy_to(pst_b[:, 0:t], ps[1][:, 0:t]))
                with act.Fori(1, KD) as d:
                    merge(l, half0(l, U_PB) + d, d + s0, gst_b, pst_b)

                def take_r(h, k):
                    u = Unit(half0(l, U_R) + h * 2, k)
                    src = ps[u.slot]
                    H = h + l * HR
                    if k < 2:
                        wait(act, k_ready, H * NLEV - (NLEV - 1))
                        take(u, copy_to(sig[:, k, :], src[:, 0:T_ALL], ACT.Sigmoid, scale=-1.0))
                    elif k == 2:
                        wait(act, lvl_mm, H * NLEV - (NLEV - 2))
                        take(u, copy_to(stq[:, 0:t], src[:, 0:t]))
                    else:
                        wait(act, v_tr, H)
                        take(u, copy_to(stv[:, :], src[:, 0:T_ALL]))

                def take_vt(h):
                    H = h + l * HR
                    wait(act, v_tr, H + 1)
                    wait(act, o_mm, H)
                    nc.scalar.activation(vt[:, :, :].rearrange("p c v -> p (c v)"), aux[:, 0:T_ALL], ACT.Copy).then_inc(vt_s, 1)

                def mix(h, n):
                    H = h + l * HR
                    m = LEVELS[n]
                    wait(act, k_ready, H * NLEV + n)
                    if n > 2:
                        wait(act, lvl_mm, H * NLEV + n - 1)
                    else:
                        wait(act, o_mm, H)
                    nc.scalar.activation(km[:, n % 2, 0:t], rows(kk, 0, [2 * m, t // (2 * m)], [T_ALL + m, 2], [1, m]), ACT.Copy).then_inc(km_s, 1)

                def take_kt(h):
                    H = h + l * HR
                    for d, o in ((0, 1024), (1, 0)):
                        wait(act, k_tr, 2 * H + d + 1)
                        wait(act, ds_mm, 2 * H)
                        nc.scalar.activation(kt[:, d, :, :].rearrange("p c v -> p (c v)"), aux[:, o:o + 5 * P], ACT.Copy).then_inc(kt_s, 1)

                def take_o(h):
                    H = h + l * HR
                    wait(act, o_mm, H + 1)
                    if not isinstance(h, int):
                        held()
                    nc.scalar.activation(ot[:, h, 0:t], aux[:, 1024:1024 + t], ACT.Copy).then_inc(o_out, 1)

                def take_cz(j):
                    u = Unit(half0(l, U_CZ), j)
                    take(u, copy_to(cz[:, j, 0:t], ps[u.slot][:, 0:t], ACT.Silu))

                if l == 1:
                    act.wait_ge(ca_l, JC)
                for k in range(4):
                    take_r(0, k)
                def recurrence(h, take_):
                    take_vt(h)
                    for n in range(1, 4):
                        mix(h, n)
                    take_(0)
                    for n in range(4, NMIX + 1):
                        mix(h, n)
                    take_(1)
                    take_(2)
                    take_kt(h)
                    take_o(h)
                    take_(3)

                with act.Fori(1, HR) as h:
                    recurrence(h - 1, lambda k: take_r(h, k))
                recurrence(HR - 1, take_cz)
                act.wait_ge(o_out, (l + 1) * HR)
                squares(i0 + 1, HR, t, sq_r, lambda k: ot[:, k, 0:t])
                take_cz(4)
                root(i0 + 1, t // 4)
                take_cz(5)
                for k in range(HR):
                    operand(2 * l * HR, k, t, ach)

                s8 = 24 * l + 8
                with act.Fori(0, JC // 2) as m:
                    for s in range(2):
                        def uu(k):
                            return Unit(half0(l, U_C) + m * 5, 5 * s + k)
                        for k, (dst, f) in enumerate(((sg, ACT.Sigmoid), (av, ACT.Copy))):
                            wait(act, u_done, m * 2 + (s + l * JC))
                            take(uu(k), copy_to(dst[:, 0:t], ps[uu(k).slot][:, 0:t], f))
                        act.wait_ge(ac_l, (l + 1) * HR)
                        act.wait_ge(unit_mm, uu(2).n + 1)
                        held()
                        nc.scalar.activation(az[:, m * 2 + s, 0:t], ps[uu(2).slot][:, 0:t], ACT.Silu).then_inc(unit_out, 1)
                        for k, (dst, f) in ((3, (gst, ACT.Sigmoid)), (4, (pst, ACT.Copy))):
                            wait(act, p_done, m * 2 + (s + s8))
                            take(uu(k), copy_to(dst[:, 0:t], ps[uu(k).slot][:, 0:t], f))
                merge(l, half0(l, U_PC), s8 + JC, gst, pst)
                u = Unit(half0(l, U_PC) + 1, 0)
                act.wait_ge(p_done, s8 + JC + 1)
                take(u, copy_to(gst[:, 0:t], ps[0][:, 0:t], ACT.Sigmoid))
                squares(i0 + 3, JC, t, sq_l, lambda k: cu[:, k, 0:t], ready=(xc_s, l * JC))
                root(i0 + 3, t // 4)
                u = Unit(half0(l, U_PC) + 1, 1)
                take(u, copy_to(pst[:, 0:t], ps[1][:, 0:t]))
                for k in range(JC + 1):
                    if k < JC:
                        act.wait_ge(lnt_s, l * JC + k + 1)
                        wait(act, tm_s, (2 * l + 1) * HR + k - 1)
                        nc.scalar.activation(lu[:, k % 2, 0:t], cu[:, k, 0:t], ACT.Silu, scale=vec[:, l * VPL + V_LG + k:l * VPL + V_LG + k + 1],
                                             bias=vec[:, l * VPL + V_LB + k:l * VPL + V_LB + k + 1]).then_inc(lu_s, 1)
                    if k > 0:
                        operand((2 * l + 1) * HR, k - 1, t, ach)

                s16 = 24 * l + 16
                merge(l, half0(l, U_PA), s16, gst, pst)
                act.wait_ge(ca_l, (l + 1) * JC)
                act.dma_start(ada_w[2][:, :, :, :], w_ada[l, 2]).then_inc(ada_full[2], 16)
                with act.Fori(1, KD) as d:
                    merge(l, half0(l, U_PA) + d, d + s16, gst, pst)
                act.dma_start(x[:, :, :], x_keep).then_inc(x_back, 16)
                for k in range(KD):
                    act.wait_ge(p_done, s16 + 8)
                    nc.scalar.activation(hh[:, k, 0:t], y[:, k, 0:t], ACT.Copy).then_inc(hf_ready, 1)
                    if k == 1:
                        ada(l, 2)
                        if l == 0:
                            for b in range(2):
                                act.dma_start(ada_w[b][:, :, :, :], w_ada[1, b]).then_inc(ada_full[b], 16)
                act.wait_ge(ada_t, 3 * l + 3)

                def take_o_unit(hb, k, dv):
                    u = Unit(hb, k)
                    wait(act, unit_mm, u.n + 1)
                    wait(act, x_ready, KD * (l + 1) + dv - 1)
                    if not isinstance(dv, int):
                        held()
                    for (i, c0, c1) in segs(t):
                        ins = nc.scalar.activation(oxs[:, k, c0:c1], ps[u.slot][:, c0:c1], ACT.Copy, scale=adat[:, 16 + dv, i:i + 1])
                    ins.then_inc(unit_out, 1)

                def square(k, dv):
                    wait(act, x_ready, KD * (l + 1) + dv + 1)
                    wait(act, sq_used, sq0[i0 + 4] + dv - 1)
                    if not isinstance(dv, int):
                        held()
                    nc.scalar.activation(sq_h[:, k, 0:t], x[:, dv, 0:t], ACT.Square).then_inc(sq_ready, 1)

                for k in range(2):
                    take_o_unit(half0(l, U_O), k, k)
                act.wait_ge(y_ready, (l + 1) * KD)
                with act.Fori(1, KD // 2 - 1) as d:
                    for k in range(2):
                        take_o_unit(half0(l, U_O) + d, k, d * 2 + k)
                        square(k, d * 2 + (k - 2))
                if l == 0:
                    for b in range(2):
                        ada(1, b)
                for k in range(2):
                    take_o_unit(half0(l, U_O) + KD // 2 - 1, k, KD - 2 + k)
                    square(k, KD - 4 + k)
                for k in range(2):
                    square(k, KD - 2 + k)
            root(8, NX // 4)
            for k in range(KD):
                act.wait_ge(y_out, k + 1)
                act.dma_start(out[:, k, :], outb[:, k, :]).then_inc(out_s, 16)
            act.wait_ge(out_s, 16 * KD)

        @block.vector
        def _(dve):
            own = Done(dve, dve_done)
            add = own.add
            tt, ts, stt = nc.vector.tensor_tensor, nc.vector.tensor_scalar, nc.vector.scalar_tensor_tensor

            def loop(a, b, per, body):
                base = own.base + own.n
                with dve.Fori(a, b) as i:
                    own.start((i - a) * per + base if per else base)
                    body(i)
                    assert own.n == per, own.n
                own.start(base + (b - a) * per)

            def ada(l, b):
                n = 3 * l + b
                dve.wait_ge(ada_tmm, n + 1)
                ins = tt(rows(adat, 16 * b, [8, 2], [2, 4], [1, 2]), rows(aux, 1536, [2, 2], [4, 4], [1, 2]),
                         rows(vec, l * VPL + V_BADA + 8 * b, [4, 2], [1, 4], [0, 2]), ALU.add)
                if b != 1:
                    add(ins, ada_t, n + 1)
                else:
                    add(ins)
                    own.all_but()
                    add(ts(coef[:, :, :], adat[:, 8:16, :], 1.0, None, ALU.add))
                    own.all_but()
                    add(tt(coef[:, :, :], coef[:, :, :], rows(vec, l * VPL + V_NORM, [1, KD], [0, 2]), ALU.mult), ada_t, n + 1)

            def variance(i, w, count, eps, root=True):
                if root:
                    dve.wait_ge(sq_used, sq0[i + 1])
                else:
                    dve.wait_ge(stat_mm, i // 4 + 1)
                add(ts(sta[:, 0:w], aux[:, 0:w], 1.0 / count, eps, ALU.mult, ALU.add), stat_v, i + 1)
                if root:
                    dve.wait_ge(stat_s, fresh(i) + 1)
                    add(nc.vector.reciprocal(stc[:, 0:w], stb[:, 0:w]), stat_r, fresh(i) + 1)

            def merge(l, hb, d, s, g_, p_, first=False):
                t = tokens(l)
                wait(dve, unit_out, Unit(hb, 1).n + 1)
                if first:
                    add(tt(y[:, d, 0:t], g_[:, 0:t], p_[:, 0:t], ALU.mult), p_done, None)
                else:
                    add(tt(p_[:, 0:t], g_[:, 0:t], p_[:, 0:t], ALU.mult))
                    own.all_but()
                    add(tt(y[:, d, 0:t], y[:, d, 0:t], p_[:, 0:t], ALU.add), p_done, None)

            add(nc.vector.memset(onecol[:, :], 0.0))
            add(nc.vector.memset(cstat[:, :, :], 0.0))
            own.all_but()
            add(nc.vector.memset(onecol[:, 32:33], 1.0), setup)
            dve.wait_ge(vec_in_s, 16)
            a_ = rows(vec, V_RLB, [12, 2], [1, 6])
            b_ = rows(vec, V_RLB + 6, [12, 2], [1, 6])
            def l2(k):
                return lbw[:, k, :].rearrange("p (d h) -> p d h", d=2)
            add(tt(l2(0), a_, b_, ALU.max))
            own.all_but()
            add(tt(l2(1), a_, l2(0), ALU.subtract))
            add(tt(l2(2), b_, l2(0), ALU.subtract), setup)
            dve.wait_ge(c_ready, 1)
            add(tt(rows(cstat, 0, [32, KD], [1, 2]), rows(ctmp, 0, [2, KD], [1, 2]), rows(vec, V_CC, [2, KD], [1, 2]), ALU.mult), lb_r)
            add(tt(lbw[:, 3, :], lbw[:, 1, :], lbw[:, 2, :], ALU.add))
            own.all_but()
            add(nc.vector.reciprocal(lbw[:, 4, :], lbw[:, 3, :]))
            own.all_but()
            add(tt(lbw[:, 5, :], lbw[:, 1, :], lbw[:, 4, :], ALU.mult))
            add(tt(lbw[:, 6, :], lbw[:, 2, :], lbw[:, 4, :], ALU.mult))
            own.all_but()
            add(tt(lbw[:, 6, :], lbw[:, 5, :], lbw[:, 6, :], ALU.add))
            own.all_but()
            add(tt(lbw[:, 6, :], lbw[:, 6, :], lbw[:, 5, :], ALU.subtract))
            add(tt(lbw[:, 7, :], lbw[:, 5, :], lbw[:, 5, :], ALU.subtract))
            own.all_but()
            for l in range(DEPTH):
                add(ts(oml[:, l, :, :], l2(7 - l), -1.0, 1.0, ALU.mult, ALU.add))
            dve.wait_ge(x_s, 16)
            dve.wait_ge(pos_s, 16)
            for k in range(KD):
                nr = NX // GRID_W
                p_ap = rows(pos, k * nr, [1, nr], [0, GRID_W]) if k < KD // 2 else rows(pos, KD // 2 * nr + (k - KD // 2) * GRID_W, [0, nr], [1, GRID_W])
                xk = x[:, k, 0:NX].rearrange("p (r c) -> p r c", c=GRID_W)
                add(tt(xk, xk, p_ap, ALU.add), x_ready)

            for l in range(DEPTH):
                t = tokens(l)
                i0 = 4 * l
                w = t // 4
                variance(i0, 192, D_MODEL, EPS)
                if l == 0:
                    for b in range(2):
                        ada(0, b)
                dve.wait_ge(bc_mm, bc0[i0] + 1)
                for k in range(KD + 1):
                    if k < KD:
                        wait(dve, hf_ready, l * 2 * KD + k - 1)
                        add(tt(quarters(ht[:, k % 2, :], 192), quarters(x[:, k, :], 192), spread(192), ALU.mult), ht_ready)
                    if k > 0:
                        dve.wait_ge(hf_ready, l * 2 * KD + k)
                        add(tt(hl[:, k - 1, :], hf[:, (k - 1) % 2, :], hh[:, k - 1, :].bitcast(F32), ALU.subtract), h_ready, l * KD + k)
                own.all_but()
                dve.sem_inc(bc_used, 1)
                for n in range(4):
                    a, b = NDFT * n // 4, NDFT * (n + 1) // 4
                    dve.wait_ge(dft_h, 4 * l + n + 1)
                    ins = tt(dcl[:, a:b], dft_raw[:, a:b], dch[:, a:b].bitcast(F32), ALU.subtract)
                    if n == 3:
                        add(ins, dft_ready, l + 1)

                def split_bu(g):
                    wait(dve, unit_out, Unit(half0(l, U_B) + g, 0).n + 1)
                    wait(dve, dft1_mm, l * GF + g)
                    add(tt(bul[:, 0:t], bur[:, 0:t], buh[:, 0:t].bitcast(F32), ALU.subtract), bulo)

                def gate_fourier(g):
                    G = l * GF + g
                    wait(dve, dft2_mm, G + 1)
                    wait(dve, abh_s, G)
                    wait(dve, abl_s, G)
                    add(tt(bt[:, 0:t], aux[:, 1024:1024 + t], bz[:, 0:t], ALU.mult), abt)
                    wait(dve, abh_s, G + 1)
                    add(tt(abl[:, g, 0:t], bt[:, 0:t], abh[:, g, 0:t].bitcast(F32), ALU.subtract), abl_s)

                def split_dft1(g):
                    n = 256 * chunks(l)
                    wait(dve, a_out, l * GF + g + 1)
                    add(tt(alo[:, 0:n], ar[:, 0:n], ahi[:, 0:n].bitcast(F32), ALU.subtract), alo_s)

                split_bu(0)
                split_dft1(0)

                def fourier(g):
                    split_bu(g)
                    gate_fourier(g - 1)
                    split_dft1(g)
                loop(1, GF, 0, fourier)
                gate_fourier(GF - 1)
                merge(l, half0(l, U_PB), 0, 24 * l, gst_b, pst_b, first=True)
                loop(1, KD, 0, lambda d: merge(l, half0(l, U_PB) + d, d, d + 24 * l, gst_b, pst_b, first=True))

                if l == 0:
                    dve.wait_ge(mask_s, 16)

                def head(h, hb_v):
                    H = h + l * HR
                    nch = chunks(l)
                    wait(dve, unit_out, hb_v * 2 - 2)
                    for d in range(2):
                        add(ts(kk[:, d, :], sig[:, d, :], oml[:, l, d, bass.ds(h, 1)] if not isinstance(h, int) else oml[:, l, d, h:h + 1],
                               K_MAX, ALU.mult, ALU.min))
                    own.all_but()
                    add(ts(ff[:, :, :], kk[:, :, :], -1.0, 1.0, ALU.mult, ALU.add))
                    add(tt(ks[:, 0:t], kk[:, 0, 0:t], kk[:, 1, 0:t], ALU.add), k_ready, H * NLEV + 1)
                    wait(dve, unit_out, hb_v * 2 - 1)
                    wait(dve, o_mm, H)
                    own.all_but(1)
                    add(tt(qq[:, :, 0:t], rows(stq, 0, [0, 2], [1, t]), ff[:, :, 0:t], ALU.mult), q_ready, H * NLEV + 1)

                    def place(n):
                        m = LEVELS[n]
                        o = 1024 if n % 2 == 0 else 0
                        wait(dve, lvl_mm, H * NLEV + n + 1)
                        if m < 32:
                            src = aux[:, o:o + nch * SUB].rearrange("p (c t) -> p c t", t=SUB)
                            dst = near[:, 0:nch * SUB].rearrange("p (c t) -> p c t", t=SUB)
                            msk = rows(masks, n * SUB, [0, nch], [1, SUB])
                            if n > 0:
                                wait(dve, lvl_used, H * (NLEV - 1) + n)
                            if m == 0:
                                add(tt(dst, src, rows(const, K_MSK, [0, nch], [1, SUB]), ALU.mult), lvl_used, H * (NLEV - 1) + n + 1)
                            else:
                                dve.sem_inc(passed["dve"], 1)
                                add(nc.vector.copy_predicated(dst, msk, src), lvl_used, H * (NLEV - 1) + n + 1)
                            if m == 16:
                                own.all_but()
                                for q in range(4):
                                    add(ts(sc[32 * q:32 * q + 32, 0:nch, 32 * q:32 * q + 32],
                                           near[32 * q:32 * q + 32, 0:nch * SUB].rearrange("p (c t) -> p c t", t=SUB), 1.0, None, ALU.mult))
                        elif m == 32:
                            for q in range(4):
                                r = q ^ 1
                                ins = ts(sc[32 * q:32 * q + 32, 0:nch, 32 * r:32 * r + 32],
                                         aux[32 * q:32 * q + 32, o:o + nch * SUB].rearrange("p (c t) -> p c t", t=SUB), 1.0, None, ALU.mult)
                            add(ins, lvl_used, H * (NLEV - 1) + n + 1)
                        else:
                            for q in range(2):
                                r = 1 - q
                                ins = ts(sc[64 * q:64 * q + 64, 0:nch, 64 * r:64 * r + 64],
                                         aux[64 * q:64 * q + 64, o:o + nch * 64].rearrange("p (c t) -> p c t", t=64), 1.0, None, ALU.mult)
                            add(ins, sc_s, H + 1)

                    def widen(n):
                        m = LEVELS[n]
                        nb = T_ALL // m
                        src = tl[m]
                        q_ap = rows(qq, m, [T_ALL - m, 2], [2 * m, t // (2 * m)], [1, m])
                        k_ap = rows(kk, 0, [T_ALL + m, 2], [2 * m, nb // 2], [1, m])
                        add(tt(k_ap, k_ap, rows(src, 1, [nb - 1, 2], [2, nb // 2], [0, m]), ALU.mult), k_ready, H * NLEV + n + 1)
                        add(tt(q_ap, q_ap, rows(src, 0, [nb + 1, 2], [2, t // (2 * m)], [0, m]), ALU.mult), q_ready, H * NLEV + n + 1)
                        add(tt(tl[2 * m][:, :, :], rows(src, 0, [nb, 2], [2, nb // 2]), rows(src, 1, [nb, 2], [2, nb // 2]), ALU.mult))

                    place(0)
                    for n in range(1, NLEV):
                        wait(dve, lvl_mm, H * NLEV + n + 1)
                        own.all_but(1)
                        widen(n)
                        place(n)
                    for n in range(5):
                        for d, order, o in ((0, FWD, 1024), (1, BWD, 0)):
                            if n == 0:
                                wait(dve, ds_mm, 2 * H + d + 1)
                                add(ts(st[:, d, 0, :], aux[:, o:o + P], 1.0, None, ALU.mult))
                            else:
                                own.all_but(1)
                                c = order[n]
                                ins = stt(st[:, d, n, :], st[:, d, n - 1, :], tl[128][:, d, c:c + 1], aux[:, o + n * P:o + (n + 1) * P], ALU.mult, ALU.add)
                                if n < 4:
                                    add(ins)
                                else:
                                    add(ins, s_ready, 2 * H + 1 + d)

                NHEAD = 3 + (NLEV - 1) + 4 + 2 * 4
                loop(0, HR, NHEAD, lambda h: head(h, h * 2 + (half0(l, U_R) + 2)))

                variance(i0 + 1, w, P, EPS)
                for k in range(HR):
                    dve.wait_ge(bc_mm, bc0[i0 + 1] + k + 1)
                    v = quarters(ot[:, k, 0:t], w)
                    add(tt(v, v, spread(w), ALU.mult), bc_used, bc0[i0 + 1] + k + 1)
                for k in range(HR + 1):
                    if k < HR:
                        dve.wait_ge(unit_out, Unit(half0(l, U_CZ), k).n + 1)
                        wait(dve, bc_used, bc0[i0 + 1] + k + 1)
                        wait(dve, ac_h, 2 * l * HR + k - 1)
                        wait(dve, ac_l, l * HR + k - 1)
                        add(stt(t1[:, k % 2, 0:t], ot[:, k, 0:t], vec[:, l * VPL + V_RG + k:l * VPL + V_RG + k + 1], cz[:, k, 0:t], ALU.mult, ALU.mult), tm_s)
                    if k > 0:
                        dve.wait_ge(ac_h, 2 * l * HR + k)
                        add(tt(acl[:, k - 1, 0:t], t1[:, (k - 1) % 2, 0:t], ach[:, k - 1, 0:t].bitcast(F32), ALU.subtract), ac_l)

                W = t + 2 * PAD if l == 0 else t
                dve.wait_ge(ac_l, (l + 1) * HR)
                add(nc.vector.memset(ub[:, :], 0.0))
                own.all_but()

                def conv(m):
                    for s in range(2):
                        j = m * 2 + s
                        hb = half0(l, U_C) + m * 5
                        wait(dve, unit_out, Unit(hb, 5 * s + 1).n + 1)
                        wait(dve, conv_done, m * 2 + (s + l * JC))
                        for (i, c0, c1) in segs(t):
                            o = PAD + (2 * PAD if i else 0)
                            ins = tt(ub[:, o + c0:o + c1], sg[:, c0:c1], av[:, c0:c1], ALU.mult)
                        ins.then_inc(u_done, 1)
                        add(ts(wj[:, 0:31], vec[:, bass.ds(m * (2 * TAPS) + (l * VPL + V_CW + s * TAPS), TAPS)], 1.0, None, ALU.mult))
                        own.all_but()
                        add(ts(acca[:, 0:W], ub[:, 0:W], wj[:, 0:1], vec[:, bass.ds(m * 2 + (l * VPL + V_CB + s), 1)], ALU.mult, ALU.add))
                        add(ts(accb[:, 0:W], ub[:, 1:1 + W], wj[:, 1:2], None, ALU.mult))
                        for k in range(2, TAPS):
                            acc = acca if k % 2 == 0 else accb
                            own.all_but(1)
                            add(stt(acc[:, 0:W], ub[:, k:k + W], wj[:, k:k + 1], acc[:, 0:W], ALU.mult, ALU.add))
                        own.all_but()
                        for (i, c0, c1) in segs(t):
                            o = 2 * PAD if i else 0
                            ins = tt(cu[:, j, c0:c1], acca[:, o + c0:o + c1], accb[:, o + c0:o + c1], ALU.add)
                        ins.then_inc(conv_done, 1)
                        wait(dve, unit_out, Unit(hb, 5 * s + 4).n + 1)
                        add(tt(pst[:, 0:t], gst[:, 0:t], pst[:, 0:t], ALU.mult))
                        own.all_but()
                        add(tt(y[:, j, 0:t], y[:, j, 0:t], pst[:, 0:t], ALU.add), p_done, None)
                ns = len(segs(t))
                loop(0, JC // 2, 2 * (1 + TAPS + 1), conv)
                s8 = 24 * l + 8
                merge(l, half0(l, U_PC), JC, s8 + JC, gst, pst)

                variance(i0 + 2, w, E_CONV, 0.0, root=False)
                dve.wait_ge(bc_mm, bc0[i0 + 2] + 1)
                for k in range(JC):
                    v = quarters(cu[:, k, 0:t], w)
                    add(tt(v, v, spread(w), ALU.subtract), xc_s, l * JC + k + 1)
                own.all_but()
                dve.sem_inc(bc_used, 1)
                variance(i0 + 3, w, E_CONV, EPS)
                dve.wait_ge(bc_mm, bc0[i0 + 3] + 1)
                for k in range(JC):
                    v = quarters(cu[:, k, 0:t], w)
                    add(tt(v, v, spread(w), ALU.mult), lnt_s, l * JC + k + 1)
                own.all_but()
                dve.sem_inc(bc_used, 1)
                merge(l, half0(l, U_PC) + 1, JC + 1, s8 + JC + 1, gst, pst)
                for k in range(JC):
                    dve.wait_ge(lu_s, l * JC + k + 1)
                    wait(dve, ac_h, (2 * l + 1) * HR + k - 1)
                    wait(dve, ca_l, l * JC + k - 1)
                    add(tt(tm[:, k % 2, 0:t], lu[:, k % 2, 0:t], az[:, k, 0:t], ALU.mult), tm_s)

                s16 = 24 * l + 16
                loop(0, KD, 1, lambda d: merge(l, half0(l, U_PA) + d, d, d + s16, gst, pst))
                for k in range(KD):
                    dve.wait_ge(hf_ready, (2 * l + 1) * KD + k + 1)
                    add(tt(hl[:, k, 0:t], y[:, k, 0:t], hh[:, k, 0:t].bitcast(F32), ALU.subtract), y_ready)
                    if k == 1:
                        ada(l, 2)
                dve.wait_ge(x_back, 16 * (l + 1))

                def residual(d):
                    for k in range(2):
                        wait(dve, unit_out, Unit(half0(l, U_O) + d, k).n + 1)
                        xd = x[:, d * 2 + k, 0:t]
                        add(tt(xd, xd, oxs[:, k, 0:t], ALU.add), x_ready)
                loop(0, KD // 2 - 1, 0, residual)
                if l == 0:
                    for b in range(2):
                        ada(1, b)
                residual(KD // 2 - 1)

            variance(8, NX // 4, D_MODEL, EPS)
            dve.wait_ge(bc_mm, bc0[8] + 1)
            own.all_but()
            w = NX // 4
            for k in range(KD):
                add(stt(quarters(outb[:, k, :], w), quarters(x[:, k, 0:NX], w), vec[:, V_FG + k:V_FG + k + 1], spread(w), ALU.mult, ALU.mult), y_out)


def _tiles(w, cols):
    n = w.shape[0] // P
    return np.stack([w[:, c:c + P].reshape(n, P, P).transpose(1, 0, 2).reshape(P, n * P) for c in cols])


def _channel_major(a):
    return a.T.reshape(-1, P, a.shape[0]).transpose(1, 0, 2)


def _columns(v):
    return v.reshape(-1, P).T


def _positions():
    rows_, quarter = NX // GRID_W, D_MODEL // 4
    omega = (1.0 / (np.float32(10000.0) ** (np.arange(quarter, dtype=np.float32) / np.float32(quarter)))).astype(np.float32)
    er = np.arange(rows_, dtype=np.float32)[:, None] * omega
    ec = np.arange(GRID_W, dtype=np.float32)[:, None] * omega
    er = np.concatenate([np.sin(er), np.cos(er)], -1)
    ec = np.concatenate([np.sin(ec), np.cos(ec)], -1)
    return np.concatenate([_channel_major(e).reshape(P, -1) for e in (er, ec)], 1).astype(np.float32)


def _fourier_matrices():
    parts = []
    for n in (NX, NCTX):
        a = 2 * np.pi * (np.outer(np.arange(n), np.arange(n)) % n) / n
        for f in (np.cos(a), -np.sin(a)):
            parts.append((f / np.sqrt(n)).reshape(n // P, P, n).transpose(1, 0, 2).reshape(P, -1))
    a = 2 * np.pi * (np.outer(np.arange(P), np.arange(P)) % P) / P
    parts += [np.cos(a) / np.sqrt(P), np.sin(a) / np.sqrt(P)]
    return np.concatenate(parts, 1).astype(np.float32)


def _small_constants():
    p, c = np.arange(P)[:, None], np.arange(P)[None]
    sub = np.arange(SUB)[None]
    sel = [np.broadcast_to((p % 32) == r, (P, P)) for r in range(6)]
    q, i = p // 32, p % 32
    asel = (i < 2) & ((q // 2) * 2 + i == np.arange(4)[None])
    const = np.concatenate([p == c, *sel, (p % 32) == sub, asel], 1).astype(np.float32)
    masks = np.zeros((P, NMASK, SUB), np.int32)
    for n in range(1, NMASK):
        m = LEVELS[n]
        masks[:, n] = ((p % 32) // (2 * m) == sub // (2 * m)) & ((p % 32) // m != sub // m)
    return const, masks


def kernel(x, c, ctx, c_ctx, w_ada, b_ada, norm_g, w_in, conv_w, conv_b, conv_ln_g, conv_ln_b,
           rec_lb, rec_norm_g, w_pa, w_pb, w_pc, w_out, final_g):
    import concourse.bacc as bacc
    from concourse.bass_utils import run_bass_kernel_spmd

    (x, c, ctx, c_ctx, w_ada, b_ada, norm_g, w_in, conv_w, conv_b, conv_ln_g, conv_ln_b, rec_lb, rec_norm_g,
     w_pa, w_pb, w_pc, w_out, final_g) = [np.asarray(a) for a in (
         x, c, ctx, c_ctx, w_ada, b_ada, norm_g, w_in, conv_w, conv_b, conv_ln_g, conv_ln_b, rec_lb, rec_norm_g,
         w_pa, w_pb, w_pc, w_out, final_g)]
    L = range(DEPTH)
    a_val, a_gate, a_z, b_u, b_z, q, f_f, f_b, i_, c_z, gates = np.cumsum([0, *[E_CONV] * 3, *[E_FOURIER] * 2, *[E_REC] * 5])
    const, masks = _small_constants()
    per_layer = [[_columns(norm_g[l]), _columns(b_ada[l]),
                  conv_w[l, :, 0].T.reshape(JC, P, TAPS).transpose(1, 0, 2).reshape(P, JC * TAPS),
                  _columns(conv_b[l]), _columns(conv_ln_g[l]), _columns(conv_ln_b[l]), _columns(rec_norm_g[l])] for l in L]
    vec = np.concatenate([v for layer in per_layer for v in layer] + [_columns(rec_lb[d, l]) for d in range(2) for l in L]
                         + [_columns(final_g), np.stack([_columns(c[0]), _columns(c_ctx)], 2).reshape(P, 2 * KD)], 1)

    def units(firsts, n):
        return np.stack([_tiles(w_in[l], [f + P * k for k in range(n) for f in firsts]) for l in L])

    arrays = {
        "x_in": np.concatenate([_channel_major(x[0]), _channel_major(ctx[0])], 2),
        "pos_in": _positions(),
        "vec_in": vec,
        "const_in": const,
        "mask_in": masks,
        "dft_in": _fourier_matrices(),
        "w_b": units([b_u, b_z], GF),
        "w_r": units([f_f, f_b, q, i_], HR),
        "w_cz": units([c_z], HR),
        "w_c": units([a_gate, a_val, a_z], JC),
        "w_g": np.stack([np.stack([_tiles(w_in[l], [gates + g * D_MODEL + P * d for d in range(KD)]) for g in range(3)]) for l in L]),
        "w_pa": np.stack([_tiles(w_pa[l], range(0, D_MODEL, P)) for l in L]),
        "w_pb": np.stack([_tiles(w_pb[l], range(0, D_MODEL, P)) for l in L]),
        "w_pc": np.stack([_tiles(w_pc[l], range(0, D_MODEL, P)) for l in L]),
        "w_o": np.stack([_tiles(w_out[l], range(0, D_MODEL, P)) for l in L]),
        "w_ada": w_ada.reshape(DEPTH, KD, P, 3, 2, ADA_W).transpose(0, 3, 2, 4, 1, 5),
    }
    arrays = {n: np.ascontiguousarray(a) for n, a in arrays.items()}
    nc = bacc.Bacc("TRN2", target_bir_lowering=False, num_devices=1)
    args = {n: nc.dram_tensor(n, a.shape, mybir.dt.from_np(a.dtype), kind="ExternalInput").ap() for n, a in arrays.items()}
    out = nc.dram_tensor("out", [P, KD, NX], F32, kind="ExternalOutput").ap()
    build(nc, *args.values(), out)
    got = run_bass_kernel_spmd(nc, [arrays], core_ids=[0]).results[0]["out"]
    return np.ascontiguousarray(got.transpose(2, 1, 0).reshape(1, NX, D_MODEL))
```

```python
from contextlib import ExitStack

import numpy as np

import concourse.bass as bass
from concourse import mybir

P = 128
D_MODEL = 1024
DEPTH = 2
NX = 512
NCTX = 256
T_ALL = NX + NCTX
GRID_W = 64
E_CONV = 768
E_FOURIER = 512
E_REC = 768
TAPS = 31
PAD = TAPS // 2
EPS = 1e-6
K_MAX = 1.0 - 1e-6

KD = D_MODEL // P
JC = E_CONV // P
GF = E_FOURIER // P
HR = E_REC // P
CHUNK = 128
SUB = 32
LEVELS = [0, 1, 2, 4, 8, 16, 32, 64]
NLEV = len(LEVELS)
NMASK = 6
NMIX = 5
ADA_W = 512
WX = T_ALL // 3

F32 = mybir.dt.float32
F32R = mybir.dt.float32r
I32 = mybir.dt.int32
ALU = mybir.AluOpType
ACT = mybir.ActivationFunctionType

VPL = 242
V_NORM, V_BADA, V_CW, V_CB, V_LG, V_LB, V_RG = 0, 8, 32, 218, 224, 230, 236
V_RLB = DEPTH * VPL
V_FG = V_RLB + 24
V_CC = V_FG + KD
NVEC = V_CC + 2 * KD

NH = NX // 2
NE = NH + 2
D_XC, D_XS = 0, 4 * NE
D_CC = D_XS + 4 * NH
D_CS = D_CC + 2 * NCTX
D_CH = D_CS + 2 * NCTX
NPOS = KD // 2 * (NX // GRID_W + GRID_W)
NDFT = D_CH + 2 * P

K_ID, K_SEL, K_MSK, K_ASEL = 0, P, 7 * P, 7 * P + SUB
NCONST = 7 * P + SUB + 4

N_B, N_PB, N_R, N_CZ, N_C, N_PC, N_PA, N_O = 2 * GF, 2 * KD, 4 * HR, HR, 5 * JC, 2 * (KD - JC), 2 * KD, KD
U_B = 0
U_PB = U_B + N_B
U_R = U_PB + N_PB
U_CZ = U_R + N_R
U_C = U_CZ + N_CZ
U_PC = U_C + N_C
U_PA = U_PC + N_PC
U_O = U_PA + N_PA
N_UNITS = U_O + N_O
KB, KC_, KA = E_FOURIER // P, E_REC // P, E_CONV // P


def build(nc, x_in, pos_in, vec_in, const_in, mask_in, dft_in, w_b, w_r, w_cz, w_c, w_g, w_pa, w_pb, w_pc, w_o, w_ada, out):
    ctx = ExitStack()
    with ctx:
        def sb(name, shape, dt=F32):
            return ctx.enter_context(nc.sbuf_tensor(name, shape, dt))

        def sem(name):
            return ctx.enter_context(nc.semaphore(name))

        hh = sb("hh", [P, KD, T_ALL], F32R)
        hl = sb("hl", [P, KD, T_ALL], F32R)
        raw = sb("raw", [P, 2, 1024])
        whi = sb("whi", [P, 2, 1024], F32R)
        wlo = sb("wlo", [P, 2, 1024], F32R)
        vec = sb("vec", [P, NVEC])
        const = sb("const", [P, NCONST])
        masks = sb("masks", [P, NMASK, SUB], I32)
        onecol = sb("onecol", [P, 64])
        cstat = sb("cstat", [P, KD, 32])
        ctmp = sb("ctmp", [P, 2 * KD])
        adat = sb("adat", [P, 24, 2])
        coef = sb("coef", [P, KD, 2])
        oml = sb("oml", [P, DEPTH, 2, HR])
        lbw = sb("lbw", [P, 8, 12])
        wj = sb("wj", [P, 32])
        sta = sb("sta", [P, WX])
        stb = sb("stb", [P, WX])
        stc = sb("stc", [P, WX])

        WORK_KB = 122
        w0 = nc.sbuf_base
        w0 = (w0 + 31) // 32 * 32
        ctx.enter_context(nc.sbuf_tensor("work_area", [P, WORK_KB * 256 + 8], F32))

        def at(name, kb, shape, dt=F32):
            t = nc.alloc_sbuf_tensor_at(name, shape, dt, offset=w0 + int(kb * 1024))
            assert int(kb * 1024) + int(np.prod(shape[1:])) * 4 <= WORK_KB * 1024, name
            return t

        y = at("y", 0, [P, KD, T_ALL])
        pos = at("pos", 0, [P, NPOS])
        sq_h = at("sq_h", 16, [P, 2, T_ALL])
        dft_raw = at("dft_raw", 0, [P, NDFT])
        bt = at("bt", 21, [P, T_ALL])
        x = at("x", 24, [P, KD, T_ALL])
        abh = at("abh", 24, [P, GF, T_ALL], F32R)
        abl = at("abl", 36, [P, GF, T_ALL], F32R)
        dch = at("dch", 48, [P, NDFT], F32R)
        dcl = at("dcl", 69, [P, NDFT], F32R)
        ada_w = [at("ada_w_shift", 56, [P, 2, KD, ADA_W]), at("ada_w_scale", 88, [P, 2, KD, ADA_W]),
                 at("ada_w_gate", 60, [P, 2, KD, ADA_W])]
        ada_row = at("ada_row", 120, [P, ADA_W])
        od = at("od", 120, [P, NH])
        ht = at("ht", 88, [P, 2, T_ALL])
        bz = at("bz", 90, [P, T_ALL])
        bur = at("bur", 93, [P, T_ALL])
        buh = at("buh", 96, [P, T_ALL], F32R)
        bul = at("bul", 99, [P, T_ALL], F32R)
        ar = at("ar", 102, [P, 6 * 2 * P])
        ahi = at("ahi", 108, [P, 6 * 2 * P], F32R)
        alo = at("alo", 114, [P, 6 * 2 * P], F32R)
        sig = at("sig", 24, [P, 2, T_ALL])
        stq = at("stq", 30, [P, T_ALL])
        stv = at("stv", 33, [P, T_ALL])
        ff = at("ff", 36, [P, 2, T_ALL])
        qq = at("qq", 42, [P, 2, T_ALL])
        kk = at("kk", 48, [P, 2, T_ALL])
        ks = at("ks", 54, [P, T_ALL])
        tl = {1: ff}
        off = 57.0
        for m in (2, 4, 8, 16, 32, 64, 128):
            tl[m] = at(f"tl{m}", off, [P, 2, T_ALL // m])
            off += 2 * T_ALL / m * 4 / 1024
        near = at("near", 63, [P, 6 * SUB])
        sc = at("sc", 64, [P, 6, CHUNK])
        vt = at("vt", 67, [P, 6, P])
        kt = at("kt", 70, [P, 2, 5, P])
        st = at("st", 75, [P, 2, 5, P])
        ot = at("ot", 80, [P, HR, T_ALL])
        km = at("km", 116, [P, 2, T_ALL])
        cz = at("cz", 98, [P, HR, T_ALL])
        ach = at("ach", 24, [P, JC, T_ALL], F32R)
        acl = at("acl", 42, [P, JC, T_ALL], F32R)
        sq_r = at("sq_r", 60, [P, 2, T_ALL])
        t1 = at("t1", 66, [P, 2, T_ALL])
        az = at("az", 60, [P, JC, T_ALL])
        cu = at("cu", 78, [P, JC, T_ALL])
        UBW = T_ALL + 4 * PAD
        ub = at("ub", 96, [P, UBW])
        acca = at("acca", 99.5, [P, UBW - 2 * PAD])
        accb = at("accb", 103, [P, UBW - 2 * PAD])
        sg = at("sg", 116, [P, T_ALL])
        av = at("av", 119, [P, T_ALL])
        sq_l = at("sq_l", 96, [P, 2, T_ALL])
        lu = at("lu", 102, [P, 2, T_ALL])
        tm = at("tm", 114, [P, 2, T_ALL])
        gst = at("gst", 108, [P, T_ALL])
        pst = at("pst", 111, [P, T_ALL])
        gst_b = at("gst_b", 102, [P, T_ALL])
        pst_b = at("pst_b", 105, [P, T_ALL])
        oxs = at("oxs", 48, [P, 2, T_ALL])
        outb = at("outb", 48, [P, KD, NX])

        ident = const[:, K_ID:K_ID + P]
        asel = const[:, K_ASEL:K_ASEL + 4]

        ps = [ctx.enter_context(nc.psum_tensor(f"unit{k}", [P, 1024], F32)) for k in range(2)]
        aux = ctx.enter_context(nc.psum_tensor("aux", [P, 2048], F32))
        x_keep = nc.dram_tensor("x_keep", [P, KD, T_ALL], F32, kind="Internal").ap()

        raw_full = [sem("raw_full0"), sem("raw_full1")]
        vec_in_s, const_s, mask_s, x_s, pos_s, dft_s = [sem(n) for n in ("vec_loaded", "const_loaded", "masks_loaded", "x_loaded", "pos_loaded", "dft_loaded")]
        ada_full = [sem("ada_shift_loaded"), sem("ada_scale_loaded"), sem("ada_gate_loaded")]
        x_kept, x_back, out_s = sem("x_kept"), sem("x_back"), sem("out_stored")
        split, rounded = sem("unit_split"), sem("weights_rounded")
        unit_mm, unit_out = sem("unit_multiplied"), sem("unit_taken_out")
        setup, c_ready, lb_r = sem("setup"), sem("c_sigmoid"), sem("c_silu_ready")
        x_ready, h_ready = sem("x_ready"), sem("h_ready")
        ada_mm, ada_rowed, ada_tmm, ada_t = sem("ada_rows_multiplied"), sem("ada_rows_out"), sem("ada_columns_multiplied"), sem("ada_ready")
        sq_ready, sq_used = sem("squares_ready"), sem("squares_summed")
        stat_mm, stat_v, stat_s, stat_r = sem("mean_summed"), sem("variance_ready"), sem("root_ready"), sem("scale_ready")
        bc_mm, bc_used = sem("scale_spread"), sem("spread_used")
        ht_ready, hf_ready = sem("normed_ready"), sem("operand_hi_ready")
        dft_h, dft_ready = sem("dft_rounded"), sem("dft_split")
        bulo, dft1_mm, a_out, alo_s = sem("bu_split"), sem("dft1_done"), sem("dft1_out"), sem("dft1_split")
        dft2_mm, abt, abh_s, abl_s = sem("dft2_done"), sem("fourier_gated"), sem("fourier_rounded"), sem("fourier_split")
        p_done, y_ready = sem("merge_done"), sem("y_split")
        v_tr, vt_s, lvl_mm, k_ready, q_ready, lvl_used = sem("v_transposed"), sem("v_rows_ready"), sem("level_multiplied"), sem("level_k_ready"), sem("level_q_ready"), sem("level_taken_out")
        k_tr, kt_s, ds_mm, s_ready, o_mm, o_out, sc_s, km_s = sem("k_transposed"), sem("k_rows_ready"), sem("state_terms_ready"), sem("states_ready"), sem("o_multiplied"), sem("o_out"), sem("scores_ready"), sem("k_mixed")
        tm_s, ac_h, ac_l, ca_l = sem("operand_ready"), sem("operand_rounded"), sem("rec_operand_split"), sem("conv_operand_split")
        u_done, conv_done = sem("conv_input_ready"), sem("conv_done")
        xc_s, lnt_s, lu_s = sem("centred"), sem("ln_scaled"), sem("ln_silu_ready")
        passed = {n: sem(f"{n}_passed") for n in ("act", "dve", "pool")}
        dve_done, act_done = sem("dve_done"), sem("act_done")
        y_out = sem("output_ready")

        def rows(t, off_, *dims, p0=0, n=P):
            width = int(np.prod(t.shape[1:]))
            return bass.AP(t, p0 * width + off_, [[width, n], *[list(d) for d in dims]])

        from_one = [s_ready, o_out, o_mm, ds_mm, u_done, abl_s, abh_s, conv_done]

        def wait(e, s, v):
            if not (isinstance(v, int) and v <= 0):
                e.wait_ge(s, v + 1 if any(s is one for one in from_one) else v)

        class Done:
            def __init__(self, e, s):
                self.e, self.s, self.base, self.n, self.signals = e, s, 0, 0, []

            def add(self, ins, s=None, v=None):
                if s is None:
                    self.n += 1
                    s, v = self.s, self.base + self.n
                self.signals.append((s, v))
                return ins.then_inc(s, 1)

            def all_but(self, lag=0):
                s, v = self.signals[-1 - lag]
                assert v is not None
                wait(self.e, s, v)

            def start(self, base):
                self.base, self.n, self.signals = base, 0, [(self.s, base), (self.s, base)]

        def tokens(l):
            return T_ALL if l == 0 else NX

        def halves(t):
            return [(0, NX), (NX, T_ALL)] if t == T_ALL else [(0, NX)]

        def segs(t):
            return [(0, 0, NX), (1, NX, T_ALL)] if t == T_ALL else [(0, 0, NX)]

        def half0(l, u):
            return (l * N_UNITS + u) // 2

        class Unit:
            def __init__(self, half, k=0):
                self.half, self.slot = half + k // 2, k % 2
                self.n = self.half * 2 + self.slot

        def chunks(l):
            return tokens(l) // CHUNK
        FWD, BWD = [4, 5, 0, 1, 2], [5, 4, 3, 2, 1]

        SQN = [8, 6, 0, 6, 8, 6, 0, 6, 8]
        BCN = [1, 6, 1, 1, 1, 6, 1, 1, 1]
        sq0 = [sum(SQN[:i]) for i in range(10)]
        bc0 = [sum(BCN[:i]) for i in range(10)]

        def fresh(i):
            return sum(1 for k in range(i) if k not in (2, 6))

        def quarters(ap2, w):
            return ap2.rearrange("p (j w) -> p j w", w=w)

        def runs(w):
            return 3 if w == WX else 4

        def spread(w):
            return aux[:, :].rearrange("p (b c) -> p b c", b=4)[:, 0:runs(w), 0:w]

        block = ctx.enter_context(nc.Block())

        @block.sync
        def _(sp):
            def load(u, src, first=False):
                n = src.shape[-1]
                if not first:
                    wait(sp, split, u.n - 1)
                sp.dma_start(raw[:, u.slot, 0:n], src).then_inc(raw_full[u.slot], 16)

            sp.dma_start(vec[:, :], vec_in).then_inc(vec_in_s, 16)
            sp.dma_start(const[:, :], const_in).then_inc(const_s, 16)
            sp.dma_start(x[:, :, :], x_in).then_inc(x_s, 16)
            sp.dma_start(pos[:, :], pos_in).then_inc(pos_s, 16)
            sp.dma_start(ada_w[0][:, :, :, :], w_ada[0, 0]).then_inc(ada_full[0], 16)
            sp.dma_start(ada_w[1][:, :, :, :], w_ada[0, 1]).then_inc(ada_full[1], 16)
            sp.dma_start(masks[:, :, :], mask_in).then_inc(mask_s, 16)
            for l in range(DEPTH):
                if l == 0:
                    for k in range(2):
                        load(Unit(0, k), w_b[0, k], first=True)
                with sp.Fori(1 if l == 0 else 0, GF) as g:
                    for k in range(2):
                        load(Unit(half0(l, U_B) + g, k), w_b[l, g * 2 + k])
                with sp.Fori(0, KD) as d:
                    load(Unit(half0(l, U_PB) + d, 0), w_g[l, 1, d])
                    load(Unit(half0(l, U_PB) + d, 1), w_pb[l, d])
                with sp.Fori(0, HR) as h:
                    for k in range(4):
                        load(Unit(half0(l, U_R) + h * 2, k), w_r[l, h * 4 + k])
                with sp.Fori(0, HR // 2) as h:
                    for k in range(2):
                        load(Unit(half0(l, U_CZ) + h, k), w_cz[l, h * 2 + k])
                with sp.Fori(0, JC // 2) as m:
                    for s in range(2):
                        for k in range(3):
                            load(Unit(half0(l, U_C) + m * 5, 5 * s + k), w_c[l, m * 6 + (3 * s + k)])
                        load(Unit(half0(l, U_C) + m * 5, 5 * s + 3), w_g[l, 2, m * 2 + s])
                        load(Unit(half0(l, U_C) + m * 5, 5 * s + 4), w_pc[l, m * 2 + s])
                for d in range(JC, KD):
                    load(Unit(half0(l, U_PC) + d - JC, 0), w_g[l, 2, d])
                    load(Unit(half0(l, U_PC) + d - JC, 1), w_pc[l, d])
                with sp.Fori(0, KD) as d:
                    load(Unit(half0(l, U_PA) + d, 0), w_g[l, 0, d])
                    load(Unit(half0(l, U_PA) + d, 1), w_pa[l, d])

                def next_ada(kc):
                    for b in range(2):
                        sp.dma_start(ada_w[b][:, :, kc, :], w_ada[1, b, :, :, kc, :]).then_inc(ada_full[b], 16)

                for k in range(2):
                    load(Unit(half0(l, U_O), k), w_o[l, k])
                if l == 0:
                    sp.wait_ge(ada_rowed, 3)
                with sp.Fori(1, KD // 2 - 1) as d:
                    for k in range(2):
                        load(Unit(half0(l, U_O) + d, k), w_o[l, d * 2 + k])
                    if l == 0:
                        for kc in range(KD // 2):
                            next_ada(d * (KD // 2) + (kc - KD // 2))
                for k in range(2):
                    load(Unit(half0(l, U_O) + KD // 2 - 1, k), w_o[l, KD - 2 + k])

        @block.gpsimd
        def _(pool):
            def split_unit(u, n=1024):
                s = u.slot
                wait(pool, raw_full[s], u.half * 16 + 16)
                wait(pool, unit_mm, u.n - 1)
                pool.sem_inc(passed["pool"], 1)
                nc.gpsimd.tensor_scalar(whi[:, s, 0:n], raw[:, s, 0:n], 1.0, 0.0, ALU.mult, ALU.add).then_inc(rounded, 1)
                wait(pool, rounded, u.n + 1)
                nc.gpsimd.tensor_tensor(wlo[:, s, 0:n], raw[:, s, 0:n], whi[:, s, 0:n].bitcast(F32), ALU.subtract).then_inc(split, 1)

            for l in range(DEPTH):
                if l == 0:
                    for k in range(2):
                        split_unit(Unit(0, k))
                with pool.Fori(1 if l == 0 else 0, GF) as g:
                    for k in range(2):
                        split_unit(Unit(half0(l, U_B) + g, k))
                with pool.Fori(0, KD) as d:
                    split_unit(Unit(half0(l, U_PB) + d, 0))
                    split_unit(Unit(half0(l, U_PB) + d, 1), KB * P)
                with pool.Fori(0, (4 * HR + HR) // 2) as h:
                    for k in range(2):
                        split_unit(Unit(half0(l, U_R) + h, k))
                with pool.Fori(0, JC // 2) as m:
                    for s in range(2):
                        for k in range(4):
                            split_unit(Unit(half0(l, U_C) + m * 5, 5 * s + k))
                        split_unit(Unit(half0(l, U_C) + m * 5, 5 * s + 4), KC_ * P)
                with pool.Fori(0, KD - JC) as d:
                    split_unit(Unit(half0(l, U_PC) + d, 0))
                    split_unit(Unit(half0(l, U_PC) + d, 1), KC_ * P)
                split_unit(Unit(half0(l, U_PA), 0))
                split_unit(Unit(half0(l, U_PA), 1), KA * P)
                for k in range(JC):
                    pool.wait_ge(ac_h, (2 * l + 1) * HR + k + 1)
                    t = tokens(l)
                    nc.gpsimd.tensor_tensor(acl[:, k, 0:t], tm[:, k % 2, 0:t], ach[:, k, 0:t].bitcast(F32), ALU.subtract).then_inc(ca_l, 1)
                with pool.Fori(1, KD) as d:
                    split_unit(Unit(half0(l, U_PA) + d, 0))
                    split_unit(Unit(half0(l, U_PA) + d, 1), KA * P)
                with pool.Fori(0, KD // 2) as d:
                    for k in range(2):
                        split_unit(Unit(half0(l, U_O) + d, k))

        @block.tensor
        def _(pe):
            pe.sem_inc(o_mm, 1)
            pe.sem_inc(ds_mm, 1)

            def begin(u):
                wait(pe, split, u.n + 1)
                wait(pe, unit_out, u.n - 1)

            def streamed_unit(u, t, nk=KD, rh=hh, rl=hl):
                wait(pe, rounded, u.n + 1)
                wait(pe, unit_out, u.n - 1)
                for last, pairs in ((False, ((whi, rh), (whi, rl))), (True, ((wlo, rh),))):
                    if last:
                        wait(pe, split, u.n + 1)
                    for kc in range(nk):
                        for n, (a, b) in enumerate(pairs):
                            for (c0, c1) in halves(t):
                                ins = nc.tensor.matmul(ps[u.slot][:, c0:c1], a[:, u.slot, kc * P:(kc + 1) * P], b[:, kc, c0:c1],
                                                       start=(kc == 0 and n == 0 and not last), stop=(last and kc == nk - 1))
                ins.then_inc(unit_mm, 1)

            def part(u, t, kcs, nk=KD, rh=hh, rl=hl, ready=None):
                ins = None
                for kc in kcs:
                    if ready is not None:
                        wait(pe, ready[0], ready[1] + kc + 1)
                    for n, (a, b) in enumerate(((whi, rh), (whi, rl), (wlo, rh))):
                        for (c0, c1) in halves(t):
                            ins = nc.tensor.matmul(ps[u.slot][:, c0:c1], a[:, u.slot, kc * P:(kc + 1) * P], b[:, kc, c0:c1],
                                                   start=(kc == 0 and n == 0), stop=(kc == nk - 1 and n == 2))
                if nk - 1 in kcs:
                    ins.then_inc(unit_mm, 1)

            def unit(u, t, nk=KD, rh=hh, rl=hl, ready=None):
                begin(u)
                part(u, t, range(nk), nk, rh, rl, ready)

            def ada_rows(l, b):
                n = 3 * l + b
                wait(pe, ada_full[b], (16 if l == 0 else 16 * (KD + 1)) if b < 2 else 16 * KD * (l + 1))
                if n == 0:
                    pe.wait_ge(setup, 1)
                    pe.wait_ge(lb_r, 1)
                wait(pe, ada_t, n)
                for k4 in range(KD // 2):
                    for q in range(4):
                        kc = (q % 2) * (KD // 2) + k4
                        ins = nc.tensor.matmul(aux[32 * q:32 * q + 32, 1536:2048], cstat[:, kc, :], ada_w[b][:, q // 2, kc, :],
                                               start=(k4 == 0), stop=(k4 == KD // 2 - 1))
                ins.then_inc(ada_mm, 1)

            def ada_columns(l, b):
                n = 3 * l + b
                pe.wait_ge(ada_rowed, n + 1)
                pe.wait_ge(const_s, 16)
                for b4 in range(4):
                    ins = nc.tensor.matmul(aux[:, 1536 + 4 * b4:1540 + 4 * b4], ada_row[:, b4 * P:(b4 + 1) * P], asel, start=True, stop=True)
                ins.then_inc(ada_tmm, 1)

            def sum_tile(k, tiles, w, src, ready, c=0, dst=aux):
                wait(pe, ready[0], ready[1] + k + 1)
                for j in range(runs(w)):
                    ins = nc.tensor.matmul(dst[32 * j:32 * j + 32, 0:w], onecol[:, 32 - c:64 - c], src[:, j * w:(j + 1) * w],
                                           start=(k == 0), stop=(k == tiles - 1))
                return ins

            def sums(i, tiles, w, src, ready, col_of=lambda k: 0, squares=True):
                wait(pe, bc_used, bc0[i])
                for k in range(tiles):
                    ins = sum_tile(k, tiles, w, src(k), ready, col_of(k))
                    if squares:
                        ins.then_inc(sq_used, 1)
                if not squares:
                    ins.then_inc(stat_mm, 1)

            def spread_rows(i, r, w, src, ready):
                wait(pe, ready[0], ready[1])
                wait(pe, bc_used, bc0[i] + r)
                for j in range(runs(w)):
                    ins = nc.tensor.matmul(aux[:, 512 * j:512 * j + w], const[32 * j:32 * j + 32, K_SEL + r * P:K_SEL + (r + 1) * P],
                                           src[32 * j:32 * j + 32, 0:w], start=True, stop=True)
                ins.then_inc(bc_mm, 1)

            def x_sums(i, w, first, n=2, stop=False):
                wait(pe, sq_ready, first + sq0[i] + n)
                for k in range(n):
                    for j in range(runs(w)):
                        ins = nc.tensor.matmul(aux[32 * j:32 * j + 32, 0:w], onecol[:, 32:64], sq_h[:, k % 2, j * w:(j + 1) * w],
                                               start=False, stop=stop and k == n - 1)
                    ins.then_inc(sq_used, 1)

            def clear_sums(i, w):
                wait(pe, bc_used, bc0[i])
                for j in range(runs(w)):
                    nc.tensor.matmul(aux[32 * j:32 * j + 32, 0:w], onecol[:, 0:32], const[:, 0:w], start=True, stop=False)

            def dft1(l, g):
                G = l * GF + g
                wait(pe, unit_out, Unit(half0(l, U_B) + g, 0).n + 1)
                wait(pe, bulo, G + 1)
                wait(pe, abt, G)
                pe.wait_ge(dft_ready, l + 1)
                for c in range(chunks(l)):
                    for n, (a, b) in enumerate(((buh, dch), (buh, dcl), (bul, dch))):
                        ins = nc.tensor.matmul(aux[:, 256 * c:256 * c + 256], a[:, c * P:(c + 1) * P], b[:, D_CH:D_CH + 2 * P], start=(n == 0), stop=(n == 2))
                ins.then_inc(dft1_mm, 1)

            def dft2(l, g):
                G = l * GF + g
                wait(pe, alo_s, G + 1)
                groups = [(1024, NE, 0, 4, ((0, D_XC),)), (1536 + NCTX, NH, 0, 4, ((1, D_XS),))]
                if l == 0:
                    groups.append((1536, NCTX, 4, 2, ((0, D_CC), (1, D_CS))))
                for (o, n, first, cnt, terms) in groups:
                    steps = [(c, p, d, q) for c in range(cnt) for (p, d) in terms for q in range(3)]
                    for (c, p, d, q) in steps:
                        a = (ahi, ahi, alo)[q]
                        b = (dch, dcl, dch)[q]
                        b0 = d + c * n
                        a0 = (first + c) * 256 + p * P
                        ins = nc.tensor.matmul(aux[:, o:o + n], a[:, a0:a0 + P], b[:, b0:b0 + n],
                                               start=((c, p, d, q) == steps[0]), stop=((c, p, d, q) == steps[-1]))
                ins.then_inc(dft2_mm, 1)

            def recurrence(l, h, us):
                t = tokens(l)
                nch = chunks(l)
                H = h + l * HR
                A, B = 0, 1024

                def level(n):
                    m = LEVELS[n]
                    o = B if n % 2 == 0 else A
                    if n > 0:
                        wait(pe, q_ready, H * NLEV + n)
                    if n == 0 or m >= 32:
                        wait(pe, k_ready, H * NLEV + max(n, 1))
                    else:
                        wait(pe, km_s, H * NMIX + n)
                    if n == 0:
                        wait(pe, o_out, H)
                    elif n == 1:
                        wait(pe, vt_s, H + 1)
                    else:
                        wait(pe, lvl_used, H * (NLEV - 1) + n - 1)
                    for c in range(nch):
                        if m < 64:
                            for q in range(4):
                                tb = c * CHUNK + q * SUB
                                dst = aux[32 * q:32 * q + 32, o + c * SUB:o + (c + 1) * SUB]
                                if m == 0:
                                    a, b = ks[:, tb:tb + SUB], stq[:, tb:tb + SUB]
                                elif m < 32:
                                    a = km[:, n % 2, tb:tb + SUB]
                                    b = rows(qq, T_ALL + tb, [2 * m, SUB // (2 * m)], [m - T_ALL, 2], [1, m])
                                elif q % 2 == 0:
                                    a, b = kk[:, 0, tb:tb + SUB], qq[:, 0, tb + SUB:tb + 2 * SUB]
                                else:
                                    a, b = kk[:, 1, tb:tb + SUB], qq[:, 1, tb - SUB:tb]
                                ins = nc.tensor.matmul(dst, a, b, start=True, stop=True)
                        else:
                            c0 = c * CHUNK
                            nc.tensor.matmul(aux[0:64, o + c * 64:o + (c + 1) * 64], kk[:, 0, c0:c0 + 64], qq[:, 0, c0 + 64:c0 + 128], start=True, stop=True)
                            ins = nc.tensor.matmul(aux[64:128, o + c * 64:o + (c + 1) * 64], kk[:, 1, c0 + 64:c0 + 128], qq[:, 1, c0:c0 + 64], start=True, stop=True)
                    ins.then_inc(lvl_mm, 1)

                todo = [(u, tt, kc) for (u, tt) in us for kc in range(KD)]

                def fill(n):
                    for _ in range(min(n, len(todo))):
                        u, tt, kc = todo.pop(0)
                        if kc == 0:
                            begin(u)
                        part(u, tt, [kc])

                fill(3)
                wait(pe, unit_out, us[0][0].n)
                wait(pe, s_ready, 2 * H)
                for c in range(6):
                    ins = nc.tensor.transpose(aux[:, A + c * P:A + (c + 1) * P], stv[:, c * P:(c + 1) * P], ident)
                ins.then_inc(v_tr, 1)
                level(0)
                fill(1)
                level(1)
                for n in range(2, NLEV):
                    fill(3)
                    level(n)
                fill(3)
                for d, order, o in ((0, FWD, B), (1, BWD, A)):
                    wait(pe, k_ready, (H + 1) * NLEV)
                    if d == 0:
                        wait(pe, lvl_used, (H + 1) * (NLEV - 1))
                    else:
                        wait(pe, sc_s, H + 1)
                    for n, c in enumerate(order):
                        ins = nc.tensor.transpose(aux[:, o + n * P:o + (n + 1) * P], kk[:, d, c * P:(c + 1) * P], ident)
                    ins.then_inc(k_tr, 1)
                fill(3)
                for d, order, o in ((0, FWD, B), (1, BWD, A)):
                    wait(pe, kt_s, 2 * H + 1 + d)
                    for n, c in enumerate(order):
                        ins = nc.tensor.matmul(aux[:, o + n * P:o + (n + 1) * P], kt[:, d, n, :], vt[:, c, :], start=True, stop=True)
                    ins.then_inc(ds_mm, 1)
                fill(3)
                wait(pe, s_ready, 2 * H + 2)
                wait(pe, sc_s, H + 1)
                for c in range(nch):
                    terms = [(vt[:, c, :], sc[:, c, :])]
                    for d, order in ((0, FWD), (1, BWD)):
                        if c != order[0]:
                            n = order.index(c) - 1 if c in order else len(order) - 1
                            terms.append((st[:, d, n, :], qq[:, d, c * P:(c + 1) * P]))
                    for n, (a, b) in enumerate(terms):
                        ins = nc.tensor.matmul(aux[:, B + c * P:B + (c + 1) * P], a, b, start=(n == 0), stop=(n == len(terms) - 1))
                ins.then_inc(o_mm, 1)
                fill(len(todo))

            class Parts:
                def __init__(self, t, units):
                    self.t = t
                    self.todo = [(u, kc, nk, rh, rl) for (u, nk, rh, rl) in units for kc in range(nk)]

                def next(self, n):
                    for u, kc, nk, rh, rl in self.todo[:n]:
                        if kc == 0:
                            begin(u)
                        part(u, self.t, [kc], nk, rh, rl)
                    self.todo = self.todo[n:]

            def merge(l, hb, nk, rh, rl):
                t = tokens(l)
                streamed_unit(Unit(hb, 0), t)
                streamed_unit(Unit(hb, 1), t, nk, rh, rl)

            for l in range(DEPTH):
                t = tokens(l)
                i0 = 4 * l
                if l == 0:
                    pe.wait_ge(setup, 1)
                    sums(0, KD, WX, lambda k: sq_h[:, k % 2, :], (sq_ready, 0))
                    for b in range(2):
                        ada_rows(0, b)
                        ada_columns(0, b)
                wait(pe, ada_t, 3 * l + 2)
                spread_rows(i0, 0, WX, stc, (stat_r, fresh(i0) + 1))
                first = [Unit(half0(l, U_B), k) for k in range(2)]
                for u in first:
                    begin(u)
                for kc in range(KD):
                    for u in first:
                        part(u, t, [kc], ready=(h_ready, l * KD))
                streamed_unit(Unit(half0(l, U_B) + 1, 0), t)
                wait(pe, bc_used, bc0[i0] + 1)
                dft1(l, 0)
                u = Unit(half0(l, U_B) + 1, 1)
                begin(u)
                part(u, t, range(0, KD // 2))
                dft2(l, 0)
                part(u, t, range(KD // 2, KD))
                dft1(l, 1)
                with pe.Fori(2, GF) as g:
                    unit(Unit(half0(l, U_B) + g, 0), t)
                    dft2(l, g - 1)
                    unit(Unit(half0(l, U_B) + g, 1), t)
                    dft1(l, g)
                streamed_unit(Unit(half0(l, U_PB), 0), t)
                dft2(l, GF - 1)
                unit(Unit(half0(l, U_PB), 1), t, KB, abh, abl, ready=(abl_s, l * GF))
                with pe.Fori(1, KD) as d:
                    merge(l, half0(l, U_PB) + d, KB, abh, abl)
                wait(pe, abt, (l + 1) * GF)
                for k in range(4):
                    unit(Unit(half0(l, U_R), k), t if k == 2 else T_ALL)
                with pe.Fori(1, HR) as h:
                    recurrence(l, h - 1, [(Unit(half0(l, U_R) + h * 2, k), t if k == 2 else T_ALL) for k in range(4)])
                recurrence(l, HR - 1, [(Unit(half0(l, U_CZ), k), t) for k in range(4)])
                w = t // 4
                cz_parts = Parts(t, [(Unit(half0(l, U_CZ), k), KD, hh, hl) for k in (4, 5)])
                cz_parts.next(1)
                wait(pe, o_out, (l + 1) * HR)
                wait(pe, bc_used, bc0[i0 + 1])
                for k in range(HR):
                    sum_tile(k, HR, w, sq_r[:, k % 2, :], (sq_ready, sq0[i0 + 1]), k).then_inc(sq_used, 1)
                    cz_parts.next(1)
                cz_parts.next(4)
                for r in range(HR):
                    spread_rows(i0 + 1, r, w, stc, (stat_r, fresh(i0 + 1) + 1))
                    cz_parts.next(1)
                with pe.Fori(0, JC // 2) as m:
                    for s in range(2):
                        for k in range(4):
                            streamed_unit(Unit(half0(l, U_C) + m * 5, 5 * s + k), t)
                        pe.wait_ge(ac_l, (l + 1) * HR)
                        streamed_unit(Unit(half0(l, U_C) + m * 5, 5 * s + 4), t, KC_, ach, acl)
                merge(l, half0(l, U_PC), KC_, ach, acl)
                sums(i0 + 2, JC, w, lambda k: cu[:, k, :], (conv_done, l * JC), squares=False)
                spread_rows(i0 + 2, 0, w, sta, (stat_v, i0 + 3))
                gate_parts = Parts(t, [(Unit(half0(l, U_PC) + 1, 0), KD, hh, hl)])
                more_parts = Parts(t, [(Unit(half0(l, U_PC) + 1, 1), KC_, ach, acl), (Unit(half0(l, U_PA), 0), KD, hh, hl)])
                wait(pe, unit_out, Unit(half0(l, U_PC) + 1, 1).n - 1)
                for k in range(JC):
                    gate_parts.next(1)
                    sum_tile(k, JC, w, sq_l[:, k % 2, :], (sq_ready, sq0[i0 + 3]), dst=ps[1]).then_inc(sq_used, 1)
                gate_parts.next(KD)
                wait(pe, stat_v, i0 + 4)
                more_parts.next(2)
                spread_rows(i0 + 3, 0, w, stc, (stat_r, fresh(i0 + 3) + 1))
                more_parts.next(KC_ + KD)
                unit(Unit(half0(l, U_PA), 1), t, KA, ach, acl, ready=(ca_l, l * JC))
                with pe.Fori(1, KD) as d:
                    merge(l, half0(l, U_PA) + d, KA, ach, acl)
                wait(pe, bc_used, bc0[i0 + 4])
                ada_rows(l, 2)
                i, w = i0 + 4, WX if l == 0 else NX // 4
                unit(Unit(half0(l, U_O), 0), t, ready=(y_ready, l * KD))
                ada_columns(l, 2)
                unit(Unit(half0(l, U_O), 1), t)
                clear_sums(i, w)
                with pe.Fori(1, KD // 2 - 1) as d:
                    for k in range(2):
                        streamed_unit(Unit(half0(l, U_O) + d, k), t)
                    x_sums(i, w, (d - 1) * 2)
                for k in range(2):
                    if l == 0:
                        ada_rows(1, k)
                    streamed_unit(Unit(half0(l, U_O) + KD // 2 - 1, k), t)
                    if l == 0:
                        ada_columns(1, k)
                x_sums(i, w, KD - 4)
                x_sums(i, w, KD - 2, n=1)
                wait(pe, sq_ready, sq0[i] + KD)
                for j in range(runs(w)):
                    ins = nc.tensor.matmul(aux[32 * j:32 * j + 32, 0:w], onecol[:, 32:64], sq_h[:, 1, j * w:(j + 1) * w], start=False, stop=True)
                ins.then_inc(sq_used, 1)
            spread_rows(8, 0, NX // 4, stc, (stat_r, fresh(8) + 1))

        @block.scalar
        def _(act):
            own = Done(act, act_done)
            act.sem_inc(o_out, 1)
            act.sem_inc(abh_s, 1)

            def take(u, *ops):
                wait(act, unit_mm, u.n + 1)
                for n, op in enumerate(ops):
                    ins = op()
                    if n == len(ops) - 1:
                        ins.then_inc(unit_out, 1)

            def copy_to(dst, src, f=ACT.Copy, **kw):
                return lambda: nc.scalar.activation(dst, src, f, **kw)

            def held():
                act.sem_inc(passed["act"], 1)

            def ada(l, b):
                n = 3 * l + b
                act.wait_ge(ada_mm, n + 1)
                wait(act, ada_tmm, n)
                nc.scalar.activation(ada_row[:, :], aux[:, 1536:2048], ACT.Copy).then_inc(ada_rowed, 1)

            def squares(i, tiles, w4, dst, src, ready=None):
                for k in range(tiles):
                    if ready is not None:
                        wait(act, ready[0], ready[1] + k + 1)
                    wait(act, sq_used, sq0[i] + k - 1)
                    nc.scalar.activation(dst[:, k % 2, 0:w4], src(k), ACT.Square).then_inc(sq_ready, 1)

            def root(i, w):
                act.wait_ge(stat_v, i + 1)
                n = 32 * runs(w)
                nc.scalar.activation(stb[0:n, 0:w], sta[0:n, 0:w], ACT.Sqrt).then_inc(stat_s, 1)

            def merge(l, hb, s, g_, p_):
                t = tokens(l)
                for k, (dst, f) in enumerate(((g_, ACT.Sigmoid), (p_, ACT.Copy))):
                    u = Unit(hb, k)
                    wait(act, p_done, s)
                    take(u, copy_to(dst[:, 0:t], ps[u.slot][:, 0:t], f))

            def operand(n0, k, t, dst_h):
                act.wait_ge(tm_s, n0 + k + 1)
                nc.scalar.activation(dst_h[:, k, 0:t], (t1 if (n0 // HR) % 2 == 0 else tm)[:, k % 2, 0:t], ACT.Copy).then_inc(ac_h, 1)

            act.wait_ge(setup, 2)
            own.add(nc.scalar.activation(lbw[:, 1, :], lbw[:, 1, :], ACT.Exp))
            own.add(nc.scalar.activation(lbw[:, 2, :], lbw[:, 2, :], ACT.Exp))
            own.all_but()
            nc.scalar.activation(ctmp[:, :], vec[:, V_CC:V_CC + 2 * KD], ACT.Sigmoid).then_inc(c_ready, 1)

            for l in range(DEPTH):
                t = tokens(l)
                i0 = 4 * l
                if l == 0:
                    squares(0, KD, T_ALL, sq_h, lambda k: x[:, k, :], ready=(x_ready, 0))
                root(i0, WX)
                if l == 0:
                    for b in range(2):
                        ada(0, b)
                act.wait_ge(sq_used, sq0[i0 + 1])
                act.wait_ge(ada_t, 3 * l + 2)
                act.dma_start(dft_raw[:, :], dft_in).then_inc(dft_s, 16)
                act.wait_ge(x_ready, (l + 1) * KD)
                act.dma_start(x_keep, x[:, :, :]).then_inc(x_kept, 16)
                for k in range(KD):
                    act.wait_ge(ht_ready, l * KD + k + 1)
                    for (i, c0, c1) in segs(T_ALL):
                        ins = nc.scalar.activation(hh[:, k, c0:c1], ht[:, k % 2, c0:c1], ACT.Identity, bias=adat[:, k, i:i + 1])
                    ins.then_inc(hf_ready, 1)
                    if k == KD - 4:
                        act.wait_ge(dft_s, 16 * (l + 1))
                    if k >= KD - 4:
                        n = k - (KD - 4)
                        a, b = NDFT * n // 4, NDFT * (n + 1) // 4
                        nc.scalar.activation(dch[:, a:b], dft_raw[:, a:b], ACT.Copy).then_inc(dft_h, 1)

                def take_bu(g):
                    u = Unit(half0(l, U_B) + g, 0)
                    wait(act, bulo, l * GF + g)
                    wait(act, dft1_mm, l * GF + g)
                    take(u, copy_to(bur[:, 0:t], ps[u.slot][:, 0:t]), copy_to(buh[:, 0:t], ps[u.slot][:, 0:t]))

                def take_bz(g):
                    u = Unit(half0(l, U_B) + g, 1)
                    wait(act, abt, l * GF + g)
                    take(u, copy_to(bz[:, 0:t], ps[u.slot][:, 0:t], ACT.Silu))

                def take_dft1(g):
                    G = l * GF + g
                    n = 256 * chunks(l)
                    wait(act, dft1_mm, G + 1)
                    wait(act, alo_s, G)
                    wait(act, dft2_mm, G)
                    nc.scalar.activation(ar[:, 0:n], aux[:, 0:n], ACT.Copy)
                    nc.scalar.activation(ahi[:, 0:n], aux[:, 0:n], ACT.Copy).then_inc(a_out, 1)

                def round_fourier(g):
                    wait(act, abt, l * GF + g + 1)
                    if not isinstance(g, int):
                        held()
                    nc.scalar.activation(abh[:, g, 0:t], bt[:, 0:t], ACT.Copy).then_inc(abh_s, 1)

                take_bu(0)
                take_bz(0)
                take_dft1(0)
                act.wait_ge(x_kept, 16 * (l + 1))
                with act.Fori(1, GF) as g:
                    take_bu(g)
                    round_fourier(g - 1)
                    take_bz(g)
                    take_dft1(g)
                s0 = 24 * l
                act.wait_ge(alo_s, (l + 1) * GF)
                u = Unit(half0(l, U_PB), 0)
                take(u, copy_to(gst_b[:, 0:t], ps[0][:, 0:t], ACT.Sigmoid))
                round_fourier(GF - 1)
                u = Unit(half0(l, U_PB), 1)
                take(u, copy_to(pst_b[:, 0:t], ps[1][:, 0:t]))
                with act.Fori(1, KD) as d:
                    merge(l, half0(l, U_PB) + d, d + s0, gst_b, pst_b)

                def take_r(h, k):
                    u = Unit(half0(l, U_R) + h * 2, k)
                    src = ps[u.slot]
                    H = h + l * HR
                    if k < 2:
                        wait(act, k_ready, H * NLEV - (NLEV - 1))
                        take(u, copy_to(sig[:, k, :], src[:, 0:T_ALL], ACT.Sigmoid, scale=-1.0))
                    elif k == 2:
                        wait(act, lvl_mm, H * NLEV - (NLEV - 2))
                        take(u, copy_to(stq[:, 0:t], src[:, 0:t]))
                    else:
                        wait(act, v_tr, H)
                        take(u, copy_to(stv[:, :], src[:, 0:T_ALL]))

                def take_vt(h):
                    H = h + l * HR
                    wait(act, v_tr, H + 1)
                    wait(act, o_mm, H)
                    nc.scalar.activation(vt[:, :, :].rearrange("p c v -> p (c v)"), aux[:, 0:T_ALL], ACT.Copy).then_inc(vt_s, 1)

                def mix(h, n):
                    H = h + l * HR
                    m = LEVELS[n]
                    wait(act, k_ready, H * NLEV + n)
                    if n > 2:
                        wait(act, lvl_mm, H * NLEV + n - 1)
                    else:
                        wait(act, o_mm, H)
                    nc.scalar.activation(km[:, n % 2, 0:t], rows(kk, 0, [2 * m, t // (2 * m)], [T_ALL + m, 2], [1, m]), ACT.Copy).then_inc(km_s, 1)

                def take_kt(h):
                    H = h + l * HR
                    for d, o in ((0, 1024), (1, 0)):
                        wait(act, k_tr, 2 * H + d + 1)
                        wait(act, ds_mm, 2 * H)
                        nc.scalar.activation(kt[:, d, :, :].rearrange("p c v -> p (c v)"), aux[:, o:o + 5 * P], ACT.Copy).then_inc(kt_s, 1)

                def take_o(h):
                    H = h + l * HR
                    wait(act, o_mm, H + 1)
                    if not isinstance(h, int):
                        held()
                    nc.scalar.activation(ot[:, h, 0:t], aux[:, 1024:1024 + t], ACT.Copy).then_inc(o_out, 1)

                def take_cz(j):
                    u = Unit(half0(l, U_CZ), j)
                    take(u, copy_to(cz[:, j, 0:t], ps[u.slot][:, 0:t], ACT.Silu))

                if l == 1:
                    act.wait_ge(ca_l, JC)
                for k in range(4):
                    take_r(0, k)
                def recurrence(h, take_):
                    take_vt(h)
                    for n in range(1, 4):
                        mix(h, n)
                    take_(0)
                    for n in range(4, NMIX + 1):
                        mix(h, n)
                    take_(1)
                    take_(2)
                    take_kt(h)
                    take_o(h)
                    take_(3)

                with act.Fori(1, HR) as h:
                    recurrence(h - 1, lambda k: take_r(h, k))
                recurrence(HR - 1, take_cz)
                wait(act, o_out, (l + 1) * HR)
                squares(i0 + 1, HR, t, sq_r, lambda k: ot[:, k, 0:t])
                root(i0 + 1, t // 4)
                take_cz(4)
                take_cz(5)
                for k in range(HR):
                    operand(2 * l * HR, k, t, ach)

                s8 = 24 * l + 8
                with act.Fori(0, JC // 2) as m:
                    for s in range(2):
                        def uu(k):
                            return Unit(half0(l, U_C) + m * 5, 5 * s + k)
                        for k, (dst, f) in enumerate(((sg, ACT.Sigmoid), (av, ACT.Copy))):
                            wait(act, u_done, m * 2 + (s + l * JC))
                            take(uu(k), copy_to(dst[:, 0:t], ps[uu(k).slot][:, 0:t], f))
                        act.wait_ge(ac_l, (l + 1) * HR)
                        act.wait_ge(unit_mm, uu(2).n + 1)
                        held()
                        nc.scalar.activation(az[:, m * 2 + s, 0:t], ps[uu(2).slot][:, 0:t], ACT.Silu).then_inc(unit_out, 1)
                        for k, (dst, f) in ((3, (gst, ACT.Sigmoid)), (4, (pst, ACT.Copy))):
                            wait(act, p_done, m * 2 + (s + s8))
                            take(uu(k), copy_to(dst[:, 0:t], ps[uu(k).slot][:, 0:t], f))
                merge(l, half0(l, U_PC), s8 + JC, gst, pst)
                squares(i0 + 3, JC, t, sq_l, lambda k: cu[:, k, 0:t], ready=(xc_s, l * JC))
                root(i0 + 3, t // 4)
                u = Unit(half0(l, U_PC) + 1, 0)
                act.wait_ge(p_done, s8 + JC + 1)
                take(u, copy_to(gst[:, 0:t], ps[0][:, 0:t], ACT.Sigmoid))
                for k in range(JC + 1):
                    if k < JC:
                        act.wait_ge(lnt_s, l * JC + k + 1)
                        wait(act, tm_s, (2 * l + 1) * HR + k - 1)
                        nc.scalar.activation(lu[:, k % 2, 0:t], cu[:, k, 0:t], ACT.Silu, scale=vec[:, l * VPL + V_LG + k:l * VPL + V_LG + k + 1],
                                             bias=vec[:, l * VPL + V_LB + k:l * VPL + V_LB + k + 1]).then_inc(lu_s, 1)
                    if k == 1:
                        u = Unit(half0(l, U_PC) + 1, 1)
                        take(u, copy_to(pst[:, 0:t], ps[1][:, 0:t]))
                    if k > 0:
                        operand((2 * l + 1) * HR, k - 1, t, ach)

                s16 = 24 * l + 16
                merge(l, half0(l, U_PA), s16, gst, pst)
                act.wait_ge(ca_l, (l + 1) * JC)

                def gate_ada(kc):
                    act.dma_start(ada_w[2][:, :, kc, :], w_ada[l, 2, :, :, kc, :]).then_inc(ada_full[2], 16)

                gate_ada(0)
                with act.Fori(1, KD) as d:
                    gate_ada(d)
                    merge(l, half0(l, U_PA) + d, d + s16, gst, pst)
                act.dma_start(x[:, :, :], x_keep).then_inc(x_back, 16)
                for k in range(KD):
                    act.wait_ge(p_done, s16 + 8)
                    nc.scalar.activation(hh[:, k, 0:t], y[:, k, 0:t], ACT.Copy).then_inc(hf_ready, 1)
                    if k == 1:
                        ada(l, 2)
                act.wait_ge(ada_t, 3 * l + 3)

                def take_o_unit(hb, k, dv):
                    u = Unit(hb, k)
                    wait(act, unit_mm, u.n + 1)
                    wait(act, x_ready, KD * (l + 1) + dv - 1)
                    if not isinstance(dv, int):
                        held()
                    for (i, c0, c1) in segs(t):
                        ins = nc.scalar.activation(oxs[:, k, c0:c1], ps[u.slot][:, c0:c1], ACT.Copy, scale=adat[:, 16 + dv, i:i + 1])
                    ins.then_inc(unit_out, 1)

                def square(k, dv):
                    wait(act, x_ready, KD * (l + 1) + dv + 1)
                    wait(act, sq_used, sq0[i0 + 4] + dv - 1)
                    if not isinstance(dv, int):
                        held()
                    nc.scalar.activation(sq_h[:, k, 0:t], x[:, dv, 0:t], ACT.Square).then_inc(sq_ready, 1)

                for k in range(2):
                    take_o_unit(half0(l, U_O), k, k)
                act.wait_ge(y_ready, (l + 1) * KD)
                with act.Fori(1, KD // 2 - 1) as d:
                    for k in range(2):
                        square(k, d * 2 + (k - 2))
                        take_o_unit(half0(l, U_O) + d, k, d * 2 + k)
                for k in range(2):
                    square(k, KD - 4 + k)
                    if l == 0:
                        ada(1, k)
                    take_o_unit(half0(l, U_O) + KD // 2 - 1, k, KD - 2 + k)
                for k in range(2):
                    square(k, KD - 2 + k)
            root(8, NX // 4)
            for k in range(KD):
                act.wait_ge(y_out, k + 1)
                act.dma_start(out[:, k, :], outb[:, k, :]).then_inc(out_s, 16)
            act.wait_ge(out_s, 16 * KD)

        @block.vector
        def _(dve):
            own = Done(dve, dve_done)
            for one in (s_ready, u_done, abl_s, conv_done):
                dve.sem_inc(one, 1)
            add = own.add
            tt, ts, stt = nc.vector.tensor_tensor, nc.vector.tensor_scalar, nc.vector.scalar_tensor_tensor

            def loop(a, b, per, body):
                base = own.base + own.n
                with dve.Fori(a, b) as i:
                    own.start((i - a) * per + base if per else base)
                    body(i)
                    assert own.n == per, own.n
                own.start(base + (b - a) * per)

            def ada(l, b):
                n = 3 * l + b
                dve.wait_ge(ada_tmm, n + 1)
                ins = tt(rows(adat, 16 * b, [8, 2], [2, 4], [1, 2]), rows(aux, 1536, [2, 2], [4, 4], [1, 2]),
                         rows(vec, l * VPL + V_BADA + 8 * b, [4, 2], [1, 4], [0, 2]), ALU.add)
                if b != 1:
                    add(ins, ada_t, n + 1)
                else:
                    add(ins)
                    own.all_but()
                    add(ts(coef[:, :, :], adat[:, 8:16, :], 1.0, None, ALU.add))
                    own.all_but()
                    add(tt(coef[:, :, :], coef[:, :, :], rows(vec, l * VPL + V_NORM, [1, KD], [0, 2]), ALU.mult), ada_t, n + 1)

            def variance(i, w, count, eps, root=True, src=aux):
                if root:
                    dve.wait_ge(sq_used, sq0[i + 1])
                else:
                    dve.wait_ge(stat_mm, i // 4 + 1)
                n = 32 * runs(w)
                add(ts(sta[0:n, 0:w], src[0:n, 0:w], 1.0 / count, eps, ALU.mult, ALU.add), stat_v, i + 1)
                if root:
                    dve.wait_ge(stat_s, fresh(i) + 1)
                    add(nc.vector.reciprocal(stc[0:n, 0:w], stb[0:n, 0:w]), stat_r, fresh(i) + 1)

            def merge(l, hb, d, s, g_, p_, first=False):
                t = tokens(l)
                wait(dve, unit_out, Unit(hb, 1).n + 1)
                if first:
                    add(tt(y[:, d, 0:t], g_[:, 0:t], p_[:, 0:t], ALU.mult), p_done, None)
                else:
                    add(tt(p_[:, 0:t], g_[:, 0:t], p_[:, 0:t], ALU.mult))
                    own.all_but()
                    add(tt(y[:, d, 0:t], y[:, d, 0:t], p_[:, 0:t], ALU.add), p_done, None)

            add(nc.vector.memset(onecol[:, :], 0.0))
            add(nc.vector.memset(cstat[:, :, :], 0.0))
            own.all_but()
            add(nc.vector.memset(onecol[:, 32:33], 1.0), setup)
            dve.wait_ge(vec_in_s, 16)
            a_ = rows(vec, V_RLB, [12, 2], [1, 6])
            b_ = rows(vec, V_RLB + 6, [12, 2], [1, 6])
            def l2(k):
                return lbw[:, k, :].rearrange("p (d h) -> p d h", d=2)
            add(tt(l2(0), a_, b_, ALU.max))
            own.all_but()
            add(tt(l2(1), a_, l2(0), ALU.subtract))
            add(tt(l2(2), b_, l2(0), ALU.subtract), setup)
            dve.wait_ge(c_ready, 1)
            add(tt(rows(cstat, 0, [32, KD], [1, 2]), rows(ctmp, 0, [2, KD], [1, 2]), rows(vec, V_CC, [2, KD], [1, 2]), ALU.mult), lb_r)
            add(tt(lbw[:, 3, :], lbw[:, 1, :], lbw[:, 2, :], ALU.add))
            own.all_but()
            add(nc.vector.reciprocal(lbw[:, 4, :], lbw[:, 3, :]))
            own.all_but()
            add(tt(lbw[:, 5, :], lbw[:, 1, :], lbw[:, 4, :], ALU.mult))
            add(tt(lbw[:, 6, :], lbw[:, 2, :], lbw[:, 4, :], ALU.mult))
            own.all_but()
            add(tt(lbw[:, 6, :], lbw[:, 5, :], lbw[:, 6, :], ALU.add))
            own.all_but()
            add(tt(lbw[:, 6, :], lbw[:, 6, :], lbw[:, 5, :], ALU.subtract))
            add(tt(lbw[:, 7, :], lbw[:, 5, :], lbw[:, 5, :], ALU.subtract))
            own.all_but()
            for l in range(DEPTH):
                add(ts(oml[:, l, :, :], l2(7 - l), -1.0, 1.0, ALU.mult, ALU.add))
            dve.wait_ge(x_s, 16)
            dve.wait_ge(pos_s, 16)
            for k in range(KD):
                nr = NX // GRID_W
                p_ap = rows(pos, k * nr, [1, nr], [0, GRID_W]) if k < KD // 2 else rows(pos, KD // 2 * nr + (k - KD // 2) * GRID_W, [0, nr], [1, GRID_W])
                xk = x[:, k, 0:NX].rearrange("p (r c) -> p r c", c=GRID_W)
                add(tt(xk, xk, p_ap, ALU.add), x_ready)

            for l in range(DEPTH):
                t = tokens(l)
                i0 = 4 * l
                w = t // 4
                variance(i0, WX, D_MODEL, EPS)
                if l == 0:
                    for b in range(2):
                        ada(0, b)
                dve.wait_ge(bc_mm, bc0[i0] + 1)
                w = WX
                for k in range(KD + 1):
                    if k < KD:
                        wait(dve, h_ready, l * KD + k - 1)
                        for (i, c0, c1) in segs(T_ALL):
                            ins = stt(quarters(ht[:, k % 2, c0:c1], w), quarters(x[:, k, c0:c1], w), coef[:, k, i:i + 1],
                                      spread(w)[:, c0 // w:c1 // w, :], ALU.mult, ALU.mult)
                        add(ins, ht_ready)
                    if k > 0:
                        dve.wait_ge(hf_ready, l * 2 * KD + k)
                        for (i, c0, c1) in segs(T_ALL):
                            ins = stt(hl[:, k - 1, c0:c1], ht[:, (k - 1) % 2, c0:c1], adat[:, k - 1, i:i + 1], hh[:, k - 1, c0:c1].bitcast(F32), ALU.add, ALU.subtract)
                        add(ins, h_ready, l * KD + k)
                w = t // 4
                own.all_but()
                dve.sem_inc(bc_used, 1)
                for n in range(4):
                    a, b = NDFT * n // 4, NDFT * (n + 1) // 4
                    dve.wait_ge(dft_h, 4 * l + n + 1)
                    ins = tt(dcl[:, a:b], dft_raw[:, a:b], dch[:, a:b].bitcast(F32), ALU.subtract)
                    if n == 3:
                        add(ins, dft_ready, l + 1)

                def split_bu(g):
                    wait(dve, unit_out, Unit(half0(l, U_B) + g, 0).n + 1)
                    wait(dve, dft1_mm, l * GF + g)
                    add(tt(bul[:, 0:t], bur[:, 0:t], buh[:, 0:t].bitcast(F32), ALU.subtract), bulo)

                def gate_fourier(g):
                    G = l * GF + g
                    wait(dve, dft2_mm, G + 1)
                    wait(dve, abh_s, G)
                    wait(dve, abl_s, G)
                    even, odd = aux[:, 1024:1024 + NH + 1], aux[:, 1536 + NCTX:1536 + NCTX + NH]
                    add(ts(od[:, :], odd, 1.0, None, ALU.mult))
                    own.all_but()
                    tt(bt[:, 0:NH], even[:, 0:NH], od[:, :], ALU.add)
                    tt(rows(bt, NX - 1, [-1, NH - 1]), even[:, 1:NH], od[:, 1:NH], ALU.subtract)
                    add(ts(bt[:, NH:NH + 1], even[:, NH:NH + 1], 1.0, None, ALU.mult))
                    if l == 0:
                        tt(bt[:, NX:T_ALL], aux[:, 1536:1536 + NCTX], bz[:, NX:T_ALL], ALU.mult)
                    own.all_but()
                    add(tt(bt[:, 0:NX], bt[:, 0:NX], bz[:, 0:NX], ALU.mult), abt)
                    wait(dve, abh_s, G + 1)
                    add(tt(abl[:, g, 0:t], bt[:, 0:t], abh[:, g, 0:t].bitcast(F32), ALU.subtract), abl_s)

                def split_dft1(g):
                    n = 256 * chunks(l)
                    wait(dve, a_out, l * GF + g + 1)
                    add(tt(alo[:, 0:n], ar[:, 0:n], ahi[:, 0:n].bitcast(F32), ALU.subtract), alo_s)

                split_bu(0)
                split_dft1(0)

                def fourier(g):
                    split_bu(g)
                    gate_fourier(g - 1)
                    split_dft1(g)
                loop(1, GF, 2, fourier)
                gate_fourier(GF - 1)
                merge(l, half0(l, U_PB), 0, 24 * l, gst_b, pst_b, first=True)
                loop(1, KD, 0, lambda d: merge(l, half0(l, U_PB) + d, d, d + 24 * l, gst_b, pst_b, first=True))

                if l == 0:
                    dve.wait_ge(mask_s, 16)

                def head(h, hb_v):
                    H = h + l * HR
                    nch = chunks(l)
                    wait(dve, unit_out, hb_v * 2 - 2)
                    for d in range(2):
                        add(ts(kk[:, d, :], sig[:, d, :], oml[:, l, d, bass.ds(h, 1)] if not isinstance(h, int) else oml[:, l, d, h:h + 1],
                               K_MAX, ALU.mult, ALU.min))
                    own.all_but()
                    add(ts(ff[:, :, :], kk[:, :, :], -1.0, 1.0, ALU.mult, ALU.add))
                    add(tt(ks[:, 0:t], kk[:, 0, 0:t], kk[:, 1, 0:t], ALU.add), k_ready, H * NLEV + 1)
                    wait(dve, unit_out, hb_v * 2 - 1)
                    wait(dve, o_mm, H)
                    own.all_but(1)
                    add(tt(qq[:, :, 0:t], rows(stq, 0, [0, 2], [1, t]), ff[:, :, 0:t], ALU.mult), q_ready, H * NLEV + 1)

                    def place(n):
                        m = LEVELS[n]
                        o = 1024 if n % 2 == 0 else 0
                        wait(dve, lvl_mm, H * NLEV + n + 1)
                        if m < 32:
                            src = aux[:, o:o + nch * SUB].rearrange("p (c t) -> p c t", t=SUB)
                            dst = near[:, 0:nch * SUB].rearrange("p (c t) -> p c t", t=SUB)
                            msk = rows(masks, n * SUB, [0, nch], [1, SUB])
                            if n > 0:
                                wait(dve, lvl_used, H * (NLEV - 1) + n)
                            if m == 0:
                                add(tt(dst, src, rows(const, K_MSK, [0, nch], [1, SUB]), ALU.mult), lvl_used, H * (NLEV - 1) + n + 1)
                            else:
                                dve.sem_inc(passed["dve"], 1)
                                add(nc.vector.copy_predicated(dst, msk, src), lvl_used, H * (NLEV - 1) + n + 1)
                            if m == 16:
                                own.all_but()
                                for q in range(4):
                                    add(ts(sc[32 * q:32 * q + 32, 0:nch, 32 * q:32 * q + 32],
                                           near[32 * q:32 * q + 32, 0:nch * SUB].rearrange("p (c t) -> p c t", t=SUB), 1.0, None, ALU.mult))
                        elif m == 32:
                            for q in range(4):
                                r = q ^ 1
                                ins = ts(sc[32 * q:32 * q + 32, 0:nch, 32 * r:32 * r + 32],
                                         aux[32 * q:32 * q + 32, o:o + nch * SUB].rearrange("p (c t) -> p c t", t=SUB), 1.0, None, ALU.mult)
                            add(ins, lvl_used, H * (NLEV - 1) + n + 1)
                        else:
                            for q in range(2):
                                r = 1 - q
                                ins = ts(sc[64 * q:64 * q + 64, 0:nch, 64 * r:64 * r + 64],
                                         aux[64 * q:64 * q + 64, o:o + nch * 64].rearrange("p (c t) -> p c t", t=64), 1.0, None, ALU.mult)
                            add(ins, sc_s, H + 1)

                    def widen(n):
                        m = LEVELS[n]
                        nb = T_ALL // m
                        src = tl[m]
                        q_ap = rows(qq, m, [T_ALL - m, 2], [2 * m, t // (2 * m)], [1, m])
                        k_ap = rows(kk, 0, [T_ALL + m, 2], [2 * m, nb // 2], [1, m])
                        add(tt(k_ap, k_ap, rows(src, 1, [nb - 1, 2], [2, nb // 2], [0, m]), ALU.mult), k_ready, H * NLEV + n + 1)
                        add(tt(q_ap, q_ap, rows(src, 0, [nb + 1, 2], [2, t // (2 * m)], [0, m]), ALU.mult), q_ready, H * NLEV + n + 1)
                        add(tt(tl[2 * m][:, :, :], rows(src, 0, [nb, 2], [2, nb // 2]), rows(src, 1, [nb, 2], [2, nb // 2]), ALU.mult))

                    place(0)
                    for n in range(1, NLEV):
                        wait(dve, lvl_mm, H * NLEV + n + 1)
                        own.all_but(1)
                        widen(n)
                        place(n)
                    for n in range(5):
                        for d, order, o in ((0, FWD, 1024), (1, BWD, 0)):
                            if n == 0:
                                wait(dve, ds_mm, 2 * H + d + 1)
                                add(ts(st[:, d, 0, :], aux[:, o:o + P], 1.0, None, ALU.mult))
                            else:
                                own.all_but(1)
                                c = order[n]
                                ins = stt(st[:, d, n, :], st[:, d, n - 1, :], tl[128][:, d, c:c + 1], aux[:, o + n * P:o + (n + 1) * P], ALU.mult, ALU.add)
                                if n < 4:
                                    add(ins)
                                else:
                                    add(ins, s_ready, 2 * H + 1 + d)

                NHEAD = 3 + (NLEV - 1) + 4 + 2 * 4
                loop(0, HR, NHEAD, lambda h: head(h, h * 2 + (half0(l, U_R) + 2)))

                variance(i0 + 1, w, P, EPS)
                for k in range(HR):
                    dve.wait_ge(bc_mm, bc0[i0 + 1] + k + 1)
                    v = quarters(ot[:, k, 0:t], w)
                    add(tt(v, v, spread(w), ALU.mult), bc_used, bc0[i0 + 1] + k + 1)
                for k in range(HR + 1):
                    if k < HR:
                        dve.wait_ge(unit_out, Unit(half0(l, U_CZ), k).n + 1)
                        wait(dve, bc_used, bc0[i0 + 1] + k + 1)
                        wait(dve, ac_h, 2 * l * HR + k - 1)
                        wait(dve, ac_l, l * HR + k - 1)
                        add(stt(t1[:, k % 2, 0:t], ot[:, k, 0:t], vec[:, l * VPL + V_RG + k:l * VPL + V_RG + k + 1], cz[:, k, 0:t], ALU.mult, ALU.mult), tm_s)
                    if k > 0:
                        dve.wait_ge(ac_h, 2 * l * HR + k)
                        add(tt(acl[:, k - 1, 0:t], t1[:, (k - 1) % 2, 0:t], ach[:, k - 1, 0:t].bitcast(F32), ALU.subtract), ac_l)

                W = t + 2 * PAD if l == 0 else t
                dve.wait_ge(ac_l, (l + 1) * HR)
                add(nc.vector.memset(ub[:, :], 0.0))
                own.all_but()

                def conv(m):
                    for s in range(2):
                        j = m * 2 + s
                        hb = half0(l, U_C) + m * 5
                        wait(dve, unit_out, Unit(hb, 5 * s + 1).n + 1)
                        wait(dve, conv_done, m * 2 + (s + l * JC))
                        for (i, c0, c1) in segs(t):
                            o = PAD + (2 * PAD if i else 0)
                            ins = tt(ub[:, o + c0:o + c1], sg[:, c0:c1], av[:, c0:c1], ALU.mult)
                        ins.then_inc(u_done, 1)
                        add(ts(wj[:, 0:31], vec[:, bass.ds(m * (2 * TAPS) + (l * VPL + V_CW + s * TAPS), TAPS)], 1.0, None, ALU.mult))
                        own.all_but()
                        add(ts(acca[:, 0:W], ub[:, 0:W], wj[:, 0:1], vec[:, bass.ds(m * 2 + (l * VPL + V_CB + s), 1)], ALU.mult, ALU.add))
                        add(ts(accb[:, 0:W], ub[:, 1:1 + W], wj[:, 1:2], None, ALU.mult))
                        for k in range(2, TAPS):
                            acc = acca if k % 2 == 0 else accb
                            own.all_but(1)
                            add(stt(acc[:, 0:W], ub[:, k:k + W], wj[:, k:k + 1], acc[:, 0:W], ALU.mult, ALU.add))
                        own.all_but()
                        for (i, c0, c1) in segs(t):
                            o = 2 * PAD if i else 0
                            ins = tt(cu[:, j, c0:c1], acca[:, o + c0:o + c1], accb[:, o + c0:o + c1], ALU.add)
                        ins.then_inc(conv_done, 1)
                        wait(dve, unit_out, Unit(hb, 5 * s + 4).n + 1)
                        add(tt(pst[:, 0:t], gst[:, 0:t], pst[:, 0:t], ALU.mult))
                        own.all_but()
                        add(tt(y[:, j, 0:t], y[:, j, 0:t], pst[:, 0:t], ALU.add), p_done, None)
                loop(0, JC // 2, 2 * (1 + TAPS + 1), conv)
                s8 = 24 * l + 8

                variance(i0 + 2, w, E_CONV, 0.0, root=False)
                dve.wait_ge(bc_mm, bc0[i0 + 2] + 1)
                for k in range(JC):
                    v = quarters(cu[:, k, 0:t], w)
                    add(tt(v, v, spread(w), ALU.subtract), xc_s, l * JC + k + 1)
                own.all_but()
                dve.sem_inc(bc_used, 1)
                merge(l, half0(l, U_PC), JC, s8 + JC, gst, pst)
                variance(i0 + 3, w, E_CONV, EPS, src=ps[1])
                dve.wait_ge(bc_mm, bc0[i0 + 3] + 1)
                for k in range(JC + 1):
                    if k < JC:
                        v = quarters(cu[:, k, 0:t], w)
                        add(tt(v, v, spread(w), ALU.mult), lnt_s, l * JC + k + 1)
                    if k == JC - 1:
                        own.all_but()
                        dve.sem_inc(bc_used, 1)
                    if k > 0:
                        j = k - 1
                        dve.wait_ge(lu_s, l * JC + j + 1)
                        wait(dve, ac_h, (2 * l + 1) * HR + j - 1)
                        wait(dve, ca_l, l * JC + j - 1)
                        add(tt(tm[:, j % 2, 0:t], lu[:, j % 2, 0:t], az[:, j, 0:t], ALU.mult), tm_s)
                merge(l, half0(l, U_PC) + 1, JC + 1, s8 + JC + 1, gst, pst)

                s16 = 24 * l + 16
                loop(0, KD, 1, lambda d: merge(l, half0(l, U_PA) + d, d, d + s16, gst, pst))
                for k in range(KD):
                    dve.wait_ge(hf_ready, (2 * l + 1) * KD + k + 1)
                    add(tt(hl[:, k, 0:t], y[:, k, 0:t], hh[:, k, 0:t].bitcast(F32), ALU.subtract), y_ready)
                ada(l, 2)
                dve.wait_ge(x_back, 16 * (l + 1))

                def residual(d, tiles=range(2)):
                    for k in tiles:
                        wait(dve, unit_out, Unit(half0(l, U_O) + d, k).n + 1)
                        xd = x[:, d * 2 + k, 0:t]
                        add(tt(xd, xd, oxs[:, k, 0:t], ALU.add), x_ready)
                loop(0, KD // 2 - 1, 0, residual)
                for k in range(2):
                    residual(KD // 2 - 1, [k])
                    if l == 0:
                        ada(1, k)

            variance(8, NX // 4, D_MODEL, EPS)
            dve.wait_ge(bc_mm, bc0[8] + 1)
            own.all_but()
            w = NX // 4
            for k in range(KD):
                add(stt(quarters(outb[:, k, :], w), quarters(x[:, k, 0:NX], w), vec[:, V_FG + k:V_FG + k + 1], spread(w), ALU.mult, ALU.mult), y_out)


def _tiles(w, cols):
    n = w.shape[0] // P
    return np.stack([w[:, c:c + P].reshape(n, P, P).transpose(1, 0, 2).reshape(P, n * P) for c in cols])


def _channel_major(a):
    return a.T.reshape(-1, P, a.shape[0]).transpose(1, 0, 2)


def _columns(v):
    return v.reshape(-1, P).T


def _positions():
    rows_, quarter = NX // GRID_W, D_MODEL // 4
    omega = (1.0 / (np.float32(10000.0) ** (np.arange(quarter, dtype=np.float32) / np.float32(quarter)))).astype(np.float32)
    er = np.arange(rows_, dtype=np.float32)[:, None] * omega
    ec = np.arange(GRID_W, dtype=np.float32)[:, None] * omega
    er = np.concatenate([np.sin(er), np.cos(er)], -1)
    ec = np.concatenate([np.sin(ec), np.cos(ec)], -1)
    return np.concatenate([_channel_major(e).reshape(P, -1) for e in (er, ec)], 1).astype(np.float32)


def _fourier_matrices():
    parts = []
    for n in (NX, NCTX):
        a = 2 * np.pi * (np.outer(np.arange(n), np.arange(n)) % n) / n
        for f, cols in ((np.cos(a), NE if n == NX else n), (-np.sin(a), NH if n == NX else n)):
            parts.append((f[:, 0:cols] / np.sqrt(n)).reshape(n // P, P, cols).transpose(1, 0, 2).reshape(P, -1))
    a = 2 * np.pi * (np.outer(np.arange(P), np.arange(P)) % P) / P
    parts += [np.cos(a) / np.sqrt(P), np.sin(a) / np.sqrt(P)]
    return np.concatenate(parts, 1).astype(np.float32)


def _small_constants():
    p, c = np.arange(P)[:, None], np.arange(P)[None]
    sub = np.arange(SUB)[None]
    sel = [np.broadcast_to((p % 32) == r, (P, P)) for r in range(6)]
    q, i = p // 32, p % 32
    asel = (i < 2) & ((q // 2) * 2 + i == np.arange(4)[None])
    const = np.concatenate([p == c, *sel, (p % 32) == sub, asel], 1).astype(np.float32)
    masks = np.zeros((P, NMASK, SUB), np.int32)
    for n in range(1, NMASK):
        m = LEVELS[n]
        masks[:, n] = ((p % 32) // (2 * m) == sub // (2 * m)) & ((p % 32) // m != sub // m)
    return const, masks


def kernel(x, c, ctx, c_ctx, w_ada, b_ada, norm_g, w_in, conv_w, conv_b, conv_ln_g, conv_ln_b,
           rec_lb, rec_norm_g, w_pa, w_pb, w_pc, w_out, final_g):
    import concourse.bacc as bacc
    from concourse.bass_utils import run_bass_kernel_spmd

    (x, c, ctx, c_ctx, w_ada, b_ada, norm_g, w_in, conv_w, conv_b, conv_ln_g, conv_ln_b, rec_lb, rec_norm_g,
     w_pa, w_pb, w_pc, w_out, final_g) = [np.asarray(a) for a in (
         x, c, ctx, c_ctx, w_ada, b_ada, norm_g, w_in, conv_w, conv_b, conv_ln_g, conv_ln_b, rec_lb, rec_norm_g,
         w_pa, w_pb, w_pc, w_out, final_g)]
    L = range(DEPTH)
    a_val, a_gate, a_z, b_u, b_z, q, f_f, f_b, i_, c_z, gates = np.cumsum([0, *[E_CONV] * 3, *[E_FOURIER] * 2, *[E_REC] * 5])
    const, masks = _small_constants()
    per_layer = [[_columns(norm_g[l]), _columns(b_ada[l]),
                  conv_w[l, :, 0].T.reshape(JC, P, TAPS).transpose(1, 0, 2).reshape(P, JC * TAPS),
                  _columns(conv_b[l]), _columns(conv_ln_g[l]), _columns(conv_ln_b[l]), _columns(rec_norm_g[l])] for l in L]
    vec = np.concatenate([v for layer in per_layer for v in layer] + [_columns(rec_lb[d, l]) for d in range(2) for l in L]
                         + [_columns(final_g), np.stack([_columns(c[0]), _columns(c_ctx)], 2).reshape(P, 2 * KD)], 1)

    def units(firsts, n):
        return np.stack([_tiles(w_in[l], [f + P * k for k in range(n) for f in firsts]) for l in L])

    arrays = {
        "x_in": np.concatenate([_channel_major(x[0]), _channel_major(ctx[0])], 2),
        "pos_in": _positions(),
        "vec_in": vec,
        "const_in": const,
        "mask_in": masks,
        "dft_in": _fourier_matrices(),
        "w_b": units([b_u, b_z], GF),
        "w_r": units([f_f, f_b, q, i_], HR),
        "w_cz": units([c_z], HR),
        "w_c": units([a_gate, a_val, a_z], JC),
        "w_g": np.stack([np.stack([_tiles(w_in[l], [gates + g * D_MODEL + P * d for d in range(KD)]) for g in range(3)]) for l in L]),
        "w_pa": np.stack([_tiles(w_pa[l], range(0, D_MODEL, P)) for l in L]),
        "w_pb": np.stack([_tiles(w_pb[l], range(0, D_MODEL, P)) for l in L]),
        "w_pc": np.stack([_tiles(w_pc[l], range(0, D_MODEL, P)) for l in L]),
        "w_o": np.stack([_tiles(w_out[l], range(0, D_MODEL, P)) for l in L]),
        "w_ada": w_ada.reshape(DEPTH, KD, P, 3, 2, ADA_W).transpose(0, 3, 2, 4, 1, 5),
    }
    arrays = {n: np.ascontiguousarray(a) for n, a in arrays.items()}
    nc = bacc.Bacc("TRN2", target_bir_lowering=False, num_devices=1)
    args = {n: nc.dram_tensor(n, a.shape, mybir.dt.from_np(a.dtype), kind="ExternalInput").ap() for n, a in arrays.items()}
    out = nc.dram_tensor("out", [P, KD, NX], F32, kind="ExternalOutput").ap()
    build(nc, *args.values(), out)
    got = run_bass_kernel_spmd(nc, [arrays], core_ids=[0]).results[0]["out"]
    return np.ascontiguousarray(got.transpose(2, 1, 0).reshape(1, NX, D_MODEL))
```
